# Optimizing a Trainium2 kernel written in Bass

```python
import jax, jax.numpy as jnp
from jax import lax
import numpy as np

D_MODEL = 1024
BATCH = 1
SEQ = 1024
DEPTH = 2

N_MEM = 256
HEAD_DIM = 64
FOX_HEADS = 8
RET_HEADS = 4
MEM_HEADS = 4
FOX_W = FOX_HEADS * HEAD_DIM
RET_W = RET_HEADS * HEAD_DIM
MEM_W = MEM_HEADS * HEAD_DIM
D_MIX = FOX_W + RET_W + MEM_W
Q_BLOCK = 128
RET_CHUNK = 128
ROPE_BASE = 10000.0
EPS = 1e-6
SPLIT_SIZES = [FOX_W, FOX_W, FOX_W, FOX_W, FOX_HEADS, RET_W, RET_W, RET_W, RET_W, MEM_W, MEM_W]
D_IN = sum(SPLIT_SIZES)
SPLIT_OFFSETS = [int(o) for o in np.cumsum(SPLIT_SIZES)[:-1]]

kernel_name = "hybrid_fox_retnet_memxattn_trunk"

def rmsnorm(x, g):
    xf = x.astype(jnp.float32)
    y = xf * lax.rsqrt(jnp.mean(xf * xf, axis=-1, keepdims=True) + EPS) * g.astype(jnp.float32)
    return y.astype(x.dtype)

def rotary(x, pos):
    d = x.shape[-1]
    half = d // 2
    freqs = ROPE_BASE ** (-jnp.arange(half, dtype=jnp.float32) / half)
    ang = pos[:, None] * freqs[None, :]
    cos, sin = jnp.cos(ang), jnp.sin(ang)
    xf = x.astype(jnp.float32)
    x1, x2 = xf[..., :half], xf[..., half:]
    return jnp.concatenate([x1 * cos - x2 * sin, x1 * sin + x2 * cos], axis=-1).astype(x.dtype)

def forgetting_attention(q, k, v, f_logit, b_f):
    B, H, S, d = q.shape
    log_f = jax.nn.log_sigmoid(f_logit.astype(jnp.float32) + b_f.astype(jnp.float32))
    c = jnp.cumsum(log_f, axis=1).transpose(0, 2, 1)
    nb = S // Q_BLOCK
    qb = q.reshape(B, H, nb, Q_BLOCK, d).transpose(2, 0, 1, 3, 4)
    cb = c.reshape(B, H, nb, Q_BLOCK).transpose(2, 0, 1, 3)
    posb = jnp.arange(S, dtype=jnp.int32).reshape(nb, Q_BLOCK)
    kpos = jnp.arange(S, dtype=jnp.int32)
    scale = d ** -0.5

    def block(args):
        qi, ci, pi = args
        s = jnp.einsum('bhqd,bhkd->bhqk', qi, k).astype(jnp.float32) * scale
        s = s + ci[..., None] - c[:, :, None, :]
        s = jnp.where(kpos[None, :] <= pi[:, None], s, -jnp.inf)
        p = jax.nn.softmax(s, axis=-1)
        return jnp.einsum('bhqk,bhkd->bhqd', p.astype(v.dtype), v)

    o = lax.map(block, (qb, cb, posb))
    return o.transpose(1, 2, 0, 3, 4).reshape(B, H, S, d)

def retention(q, k, v):
    B, H, S, d = q.shape
    C = RET_CHUNK
    N = S // C
    pos = jnp.arange(S, dtype=jnp.float32)
    q = rotary(q, pos)
    k = rotary(k, pos) * (d ** -0.5)
    log_gamma = jnp.log(1.0 - 2.0 ** (-5.0 - jnp.arange(H, dtype=jnp.float32)))
    idx = jnp.arange(C, dtype=jnp.float32)
    diff = idx[:, None] - idx[None, :]
    decay_intra = jnp.where(diff >= 0, jnp.exp(log_gamma[:, None, None] * jnp.maximum(diff, 0.0)), 0.0)
    zeta = jnp.exp(log_gamma[:, None] * (C - 1 - idx)[None, :])
    xi = jnp.exp(log_gamma[:, None] * (idx + 1)[None, :])
    decay_chunk = jnp.exp(log_gamma * C)[None, :, None, None]

    qc = q.reshape(B, H, N, C, d)
    kc = k.reshape(B, H, N, C, d)
    vc = v.reshape(B, H, N, C, d)
    a = jnp.einsum('bhncd,bhnmd->bhncm', qc, kc) * decay_intra[None, :, None]
    o_intra = jnp.einsum('bhncm,bhnme->bhnce', a, vc)
    kv = jnp.einsum('bhnmd,bhnme->bhnde', kc * zeta[None, :, None, :, None], vc)
    kv_seq = jnp.moveaxis(kv, 2, 0)

    def step(R, kv_i):
        return decay_chunk * R + kv_i, R

    _, R_prev = lax.scan(step, jnp.zeros_like(kv_seq[0]), kv_seq)
    R_prev = jnp.moveaxis(R_prev, 0, 2)
    o_cross = jnp.einsum('bhncd,bhnde->bhnce', qc * xi[None, :, None, :, None], R_prev)
    o = (o_intra + o_cross).reshape(B, H, S, d)
    of = o.astype(jnp.float32)
    of = of * lax.rsqrt(jnp.mean(of * of, axis=-1, keepdims=True) + EPS)
    return of.astype(v.dtype)

def memory_attention(q, mem, w_mkv, g_mem):
    B, H, S, d = q.shape
    mh = rmsnorm(mem, g_mem)
    kv = jnp.einsum('bmd,de->bme', mh, w_mkv)
    mk, mv = jnp.split(kv, 2, axis=-1)
    M = mem.shape[1]
    mk = mk.reshape(B, M, H, d)
    mv = mv.reshape(B, M, H, d)
    s = jnp.einsum('bhsd,bmhd->bhsm', q, mk).astype(jnp.float32) * (d ** -0.5)
    p = jax.nn.softmax(s, axis=-1)
    return jnp.einsum('bhsm,bmhd->bhsd', p.astype(mv.dtype), mv)

def hybrid_layer(x, mem, w_in, b_f, w_out, w_mkv, g_pre, g_post, g_mem):
    B, S, _ = x.shape
    h = rmsnorm(x, g_pre)
    p = jnp.einsum('bsd,de->bse', h, w_in)
    fq, fk, fv, fz, ff, rq, rk, rv, rz, mq, mz = jnp.split(p, SPLIT_OFFSETS, axis=-1)

    def heads(t, H):
        return t.reshape(B, S, H, HEAD_DIM).transpose(0, 2, 1, 3)

    def merge(t):
        return t.transpose(0, 2, 1, 3).reshape(B, S, -1)

    fox = forgetting_attention(heads(fq, FOX_HEADS), heads(fk, FOX_HEADS), heads(fv, FOX_HEADS), ff, b_f)
    ret = retention(heads(rq, RET_HEADS), heads(rk, RET_HEADS), heads(rv, RET_HEADS))
    mxa = memory_attention(heads(mq, MEM_HEADS), mem, w_mkv, g_mem)
    y = jnp.concatenate([
        merge(fox) * jax.nn.silu(fz),
        merge(ret) * jax.nn.silu(rz),
        merge(mxa) * jax.nn.silu(mz),
    ], axis=-1)
    o = jnp.einsum('bse,ed->bsd', y, w_out)
    return x + rmsnorm(o, g_post)

def setup_inputs(seed: int = 0) -> dict:
    key = jax.random.key(seed)
    ks = jax.random.split(key, 10)
    f32 = jnp.float32
    x = jax.random.normal(ks[0], (BATCH, SEQ, D_MODEL), f32)
    mem = jax.random.normal(ks[1], (BATCH, N_MEM, D_MODEL), f32)
    w_in = jax.random.normal(ks[2], (DEPTH, D_MODEL, D_IN), f32) * D_MODEL ** -0.5
    b_f = jnp.linspace(1.0, 5.0, FOX_HEADS, dtype=f32)[None, :] + 0.1 * jax.random.normal(ks[3], (DEPTH, FOX_HEADS), f32)
    w_out = jax.random.normal(ks[4], (DEPTH, D_MIX, D_MODEL), f32) * D_MIX ** -0.5
    w_mem_kv = jax.random.normal(ks[5], (DEPTH, D_MODEL, 2 * MEM_W), f32) * D_MODEL ** -0.5
    pre_norm = 1.0 + 0.02 * jax.random.normal(ks[6], (DEPTH, D_MODEL), f32)
    post_norm = 1.0 + 0.02 * jax.random.normal(ks[7], (DEPTH, D_MODEL), f32)
    mem_norm = 1.0 + 0.02 * jax.random.normal(ks[8], (DEPTH, D_MODEL), f32)
    return {"x": x, "mem": mem, "w_in": w_in, "b_f": b_f, "w_out": w_out,
            "w_mem_kv": w_mem_kv, "pre_norm": pre_norm, "post_norm": post_norm,
            "mem_norm": mem_norm}

def reference(x, mem, w_in, b_f, w_out, w_mem_kv, pre_norm, post_norm, mem_norm):
    for i in range(DEPTH):
        x = hybrid_layer(x, mem, w_in[i], b_f[i], w_out[i], w_mem_kv[i],
                         pre_norm[i], post_norm[i], mem_norm[i])
    return x


_drawn_inputs = setup_inputs


def setup_inputs(seed=0):
    import zlib

    import numpy as np

    out = dict(_drawn_inputs(seed))
    spreads = {}
    factors = {'mem_norm': 8.0}
    for name, (base, spread) in spreads.items():
        noise = np.random.default_rng([zlib.crc32(name.encode()), seed]).standard_normal(out[name].shape)
        drawn = base * np.exp(spread * noise) if base else spread * noise
        out[name] = __import__('jax').numpy.asarray(drawn.astype(out[name].dtype))
    for name, factor in factors.items():
        out[name] = (out[name] * factor).astype(out[name].dtype)
    return out
```

```python
from contextlib import ExitStack

import concourse.bass as bass
from concourse import mybir

F32 = mybir.dt.float32
F16 = mybir.dt.float16
BF16 = mybir.dt.bfloat16
I32 = mybir.dt.int32
ALU = mybir.AluOpType
ACT = mybir.ActivationFunctionType
AX = mybir.AxisListType
RMAX = bass.bass_isa.ReduceOp.max

P = 128
D = 1024
S = 1024
DEPTH = 2
HD = 64
N_MEM = 256
FOX, RET, MEM = 8, 4, 4
EPS = 1e-6
ND = D // P
NT = S // P
NMT = N_MEM // P
HALF = S // 512

FOX_W, RET_W, MEM_W = FOX * HD, RET * HD, MEM * HD
C_FF = 4 * FOX_W
C_RQ = C_FF + FOX
C_RK = C_RQ + RET_W
C_RZ = C_RK + 2 * RET_W
C_MQ = C_RZ + RET_W
C_MZ = C_MQ + MEM_W

MKV, FFRQ, RKRV, RZ, MQ, MZ, FQ, FK, FV, FZ, WO0, WO1 = range(12)
G_PRE, G_MEM, G_ONE = range(3)
CHUNKS = [(2 * MEM_W, 0, G_MEM), (FOX + RET_W, C_FF, G_PRE), (2 * RET_W, C_RK, G_PRE), (RET_W, C_RZ, G_PRE),
          (MEM_W, C_MQ, G_PRE), (MEM_W, C_MZ, G_PRE), (FOX_W, 0, G_PRE), (FOX_W, FOX_W, G_PRE),
          (FOX_W, 2 * FOX_W, G_PRE), (FOX_W, 3 * FOX_W, G_PRE), (512, 0, G_ONE), (512, 512, G_ONE)]
NCH = len(CHUNKS)

_USES = [("mk", 2), ("mv", NMT), ("ffrq", NT), ("rkrv", NT), ("rz", NT), ("mq", 4), ("mo", MEM), ("mz", NT),
         ("fq", 8), ("fk", 8), ("fv", NT), ("fo", FOX), ("fz", NT), ("wo0", NT), ("wo1", NT)]
PJ = {}
N_PJ = 0
for _n, _c in _USES:
    PJ[_n] = N_PJ
    N_PJ += _c
assert N_PJ % 2 == 0

TR_NORM = 0
TR_RET = TR_NORM + 2 * (NMT + NT)
TR_F = TR_RET + 2 * NT
TR_ATT = TR_F + 2

ITEMS = [(0, h, t, NMT) for h in range(MEM) for t in range(NT)] + \
        [(1, h, t, t + 1) for h in range(FOX) for t in range(NT)]
N_MI = MEM * NT
N_IT = len(ITEMS)
ITEM_TR = []
_u = TR_ATT
for _it in ITEMS:
    ITEM_TR.append(list(range(_u, _u + (_it[3] + 3) // 4)))
    _u += (_it[3] + 3) // 4
TR_Y = _u
N_TR = TR_Y + 2 * NT
assert N_TR % 2 == 0 and N_IT % 2 == 0

CR = 2


def n_full(u):
    return u - min(max(u - PJ["mo"], 0), MEM) - min(max(u - PJ["fo"], 0), FOX)


N_FULL = n_full(N_PJ)


def n_hi(u):
    return u - min(max(u - TR_RET, 0), TR_ATT - TR_RET)


N_HI = n_hi(N_TR)
SPLIT = [PJ["mk"], PJ["mk"] + 1] + [PJ["mv"] + i for i in range(NMT)] + [PJ["mq"] + i for i in range(4)] + \
        [PJ["fq"] + i for i in range(8)] + [PJ["fk"] + i for i in range(8)] + [PJ["fv"] + i for i in range(NT)]
N_SPLIT = len(SPLIT)
NAT = [(PJ["mk"] + i, 8) for i in range(2)] + [(PJ["mq"] + i, 4) for i in range(4)] + \
      [(PJ["fq"] + i, 4) for i in range(8)] + [(PJ["fk"] + i, 8) for i in range(8)]
NAT_AT = {u: v for v, (u, _) in enumerate(NAT)}
NAT_LAYER = 16 * sum(n for v, (_, n) in enumerate(NAT) if v % 2 == 0)
assert NAT_LAYER == 16 * sum(n for v, (_, n) in enumerate(NAT) if v % 2 == 1)


def nat_count(u):
    v = NAT_AT[u]
    return 16 * sum(n for w, (_, n) in enumerate(NAT) if w <= v and w % 2 == v % 2)


N_Z = 3 * NT
N_SS = NMT + 2 * NT


def build(nc, x, mem, w_in, b_f, w_out, w_mkv, g_pre, g_post, g_mem, tables, out):
    ctx = ExitStack()
    with ctx:
        def sb(name, shape, dt=F32):
            return ctx.enter_context(nc.sbuf_tensor(name, shape, dt))

        def sem(name):
            return ctx.enter_context(nc.semaphore(name))

        hT = sb("hT", [P, 2, ND, S], F16)
        stage = sb("stage", [P, ND, 512])
        wp = sb("wp", [P, 2, 2, ND, 512], F16)
        y = sb("y", [P, NT, D])
        cb = sb("cb", [P, 2, S])
        tp = sb("tp", [P, 3, S])
        pt = sb("pt", [P, 2, 2, S], F16)
        region = sb("region", [P, 16384])
        tab = sb("tab", [P, 140])
        msk = sb("msk", [P, 2, P], BF16)
        fcol = sb("fcol", [P, NT, FOX])
        fabs = sb("fabs", [P, NT, FOX])
        gcol = sb("gcol", [P, 3, ND])
        gabs = sb("gabs", [P, 3, ND])
        bfb = sb("bfb", [P, FOX])
        rmax = sb("rmax", [P, ND])
        pmax = sb("pmax", [P, 1])
        amax = sb("amax", [P, 1])
        sval = sb("sval", [P, NCH])
        unsc = sb("unsc", [P, NCH])
        gs = sb("gs", [P, 2, ND])
        ssq = sb("ssq", [P, N_SS])
        msq = sb("msq", [P, N_SS])
        rstd = sb("rstd", [P, N_SS])
        negh = sb("negh", [P, 4])
        ones1 = sb("ones1", [P, 1])
        gss = sb("gss", [P, NT, 4])
        gms = sb("gms", [P, NT, 4])
        gnr = sb("gnr", [P, NT, 4])
        sc2 = sb("sc2", [P, 2, 3])
        mx = sb("mx", [P, 4])
        nm = sb("nm", [P, 4])
        rs = sb("rs", [P, 2, NT])
        rec = sb("rec", [P, 2, NT])
        ymax = sb("ymax", [P, NT])
        ysc = sb("ysc", [P, NT])
        yun = sb("yun", [P, NT])
        fo = sb("fo", [P, 2, NT])

        zeta_c, xi_c, dc_c = tab[:, 0:4], tab[:, 4:8], tab[:, 8:12]
        ident = tab[:, 12:140]
        ident_b, mask_b = msk[:, 0, :], msk[:, 1, :]

        def words(a, n, rows=P):
            return region[0:rows, a:a + n]

        xin = words(0, 8192).rearrange("p (t n) -> p t n", t=NT)
        memin = words(14336, 2048).rearrange("p (t n) -> p t n", t=NMT)
        rtab = words(0, 1024)
        cos_t, sin_t, decay_t = rtab[:, 0:256], rtab[:, 256:512], rtab[:, 512:1024]
        memT = words(12288, 2048).bitcast(F16).rearrange("p (a t n) -> p a t n", a=2, t=ND)
        qr = words(2048, 2048).rearrange("p (t n) -> p t n", t=NT)
        kr = words(4096, 512).rearrange("p (a n) -> p a n", a=2)
        kz = words(4608, 512).rearrange("p (a n) -> p a n", a=2)
        rv = words(5120, 512).rearrange("p (a n) -> p a n", a=2)
        rot = words(5632, 512).rearrange("p (a n) -> p a n", a=2)
        qkT = words(6144, 2048, HD).rearrange("p (a b n) -> p a b n", a=2, b=2)
        aT = words(8192, 1024).rearrange("p (a n) -> p a n", a=2)
        rcr = words(9216, 256)
        rsq = words(9472, 256)
        junk = words(9728, 1024)
        state = words(10752, 512, HD).rearrange("p (a n) -> p a n", a=2)
        ro = words(11264, 512).rearrange("p (a n) -> p a n", a=2)
        rst = words(11776, 256, HD)
        crow = words(8192, 1024, FOX)
        mqst = words(13056, 2048).bitcast(F16).rearrange("p (h n) -> p h n", h=MEM)
        mkst = words(15104, 1024).bitcast(F16).rearrange("p (h a n) -> p h a n", h=MEM, a=2)
        mvs = words(9728, 512).bitcast(F16).rearrange("p (a t n) -> p a t n", a=2, t=NMT)
        qst = words(0, 4096).bitcast(F16).rearrange("p (h n) -> p h n", h=FOX)
        kst = words(4096, 8192).bitcast(F16).rearrange("p (h a n) -> p h a n", h=FOX, a=2)
        fvs = words(12288, 4096).bitcast(F16).rearrange("p (a t n) -> p a t n", a=2, t=NT)
        ost = xin
        gpost = cb[:, 0, :]
        mzero = cb[:, 0, 0:N_MEM]

        pj = ctx.enter_context(nc.psum_tensor("pj", [P, 2, 512], F32))
        tr = ctx.enter_context(nc.psum_tensor("tr", [P, 2, 512], F32))
        sp = ctx.enter_context(nc.psum_tensor("sp", [P, 2, S], F32))
        ret_a, ret_o, ret_kv = sp[:, 0, 0:512], sp[:, 0, 512:1024], sp[0:HD, 1, 0:256]

        def tr_bank(u):
            if TR_ATT <= u < TR_Y:
                k = (u - TR_ATT) % 3
                return pj[:, 1, :] if k == 2 else tr[:, k, :]
            return tr[:, u % 2, :]

        cdram = nc.dram_tensor("c_rows", (FOX, S), F32, kind="Internal").ap()

        held = sem("held")
        tab_in = sem("tab_in")
        w_in_sb = sem("w_in_sb")
        g_in = sem("g_in")
        gp_in = sem("gp_in")
        x_in = [sem(f"x_in{s}") for s in range(NT)]
        mem_in = sem("mem_in")
        rtab_in = sem("rtab_in")
        xr_in = [sem("xr_in0"), sem("xr_in1")]
        st_out = [sem("st_out0"), sem("st_out1")]
        stk_in = [sem("stk_in0"), sem("stk_in1")]
        c_out = sem("c_out")
        cb_in = [sem("cb_in0"), sem("cb_in1")]
        consts = sem("consts")
        gabs_ok = sem("gabs_ok")
        amax_p = sem("amax_p")
        amax_a = sem("amax_a")
        w_scale = sem("w_scale")
        w_hi = sem("w_hi")
        w_ok = sem("w_ok")
        ss_ok = sem("ss_ok")
        rstd_ok = sem("rstd_ok")
        xh_ok = sem("xh_ok")
        pj_full = sem("pj_full")
        pj_hi = sem("pj_hi")
        pj_free = sem("pj_free")
        silu_ok = sem("silu_ok")
        tr_full = sem("tr_full")
        tr_hi = sem("tr_hi")
        tr_free = sem("tr_free")
        kr_ok = sem("kr_ok")
        ra_full = sem("ra_full")
        ra_ok = sem("ra_ok")
        rkv_full = sem("rkv_full")
        state_ok = sem("state_ok")
        ro_full = sem("ro_full")
        ro_free = sem("ro_free")
        gss_ok = sem("gss_ok")
        gnr_ok = sem("gnr_ok")
        fa_ok = sem("fa_ok")
        fl_ok = sem("fl_ok")
        fe_ok = sem("fe_ok")
        lf_ok = sem("lf_ok")
        crow_ok = sem("crow_ok")
        s_full = sem("s_full")
        s_free = sem("s_free")
        nm_ok = sem("nm_ok")
        p_ok = sem("p_ok")
        pv_done = sem("pv_done")
        ys_ok = sem("ys_ok")
        o_ok = sem("o_ok")
        out_ok = sem("out_ok")

        def chunk_src(l, c):
            width, c0, _ = CHUNKS[c]
            w = w_mkv if c == MKV else (w_out if c >= WO0 else w_in)
            return w.rearrange("l (p t) n -> l p t n", p=P)[l, :, :, c0:c0 + width]

        x_rows = x.rearrange("b (t p) d -> (b t) p d", p=P)
        mem_rows = mem.rearrange("b (t p) d -> (b t) p d", p=P)
        out_rows = out.rearrange("b (t p) d -> (b t) p d", p=P)

        def norm_rows(j):
            return xin[:, j, :] if j < NT else memin[:, j - NT, :]

        def norm_dst(j):
            t = j if j < NT else j - NT
            return (hT if j < NT else memT), slice(t * P, t * P + P)

        block = ctx.enter_context(nc.Block())

        @block.sync
        def _(q):
            def load_w(l, c):
                q.wait_ge(w_ok, l * NCH + c + 1)
                q.sem_inc(held, 1)
                q.dma_start(stage[:, :, 0:CHUNKS[c][0]], chunk_src(l, c)).then_inc(w_in_sb, 16)

            def spread(l, u, dst, k_like, head0, s0, n):
                slot = NAT_AT[u] % 2
                q.wait_ge(pj_free, l * N_PJ + u + 1 + CR)
                for b in range(2):
                    rows = slice(HD * b, HD * b + HD)
                    hi, lo = pt[rows, slot, 0, 0:n], pt[rows, slot, 1, 0:n]
                    h = head0 + b
                    if k_like:
                        for a, part in ((0, hi), (1, lo)):
                            for r in range(2):
                                q.dma_start(dst[HD * r:HD * r + HD, h, a, s0:s0 + n], part).then_inc(stk_in[slot], 16)
                    else:
                        q.dma_start(dst[0:HD, h, s0:s0 + n], hi).then_inc(stk_in[slot], 16)
                        q.dma_start(dst[HD:P, h, s0:s0 + n], lo).then_inc(stk_in[slot], 16)

            for s in range(NT):
                q.dma_start(xin[:, s, :], x_rows[s]).then_inc(x_in[s], 16)
                if s == 1:
                    q.dma_start(tab[:], tables[:, 0:140]).then_inc(tab_in, 16)
            q.dma_start(out_rows[0:NT // 2], x_rows[0:NT // 2]).then_inc(st_out[0], 16)
            q.dma_start(out_rows[NT // 2:NT], x_rows[NT // 2:NT]).then_inc(st_out[1], 16)
            with q.Fori(0, DEPTH) as l:
                q.dma_start(memin, mem.rearrange("b (t p) d -> p (b t) d", p=P)).then_inc(mem_in, 16)
                load_w(l, MKV)
                for g, src in ((G_PRE, g_pre), (G_MEM, g_mem)):
                    q.dma_start(gcol[:, g, :], src.rearrange("l (p t) -> l p t", p=P)[l]).then_inc(g_in, 16)
                q.dma_start(bfb[:], b_f[l].partition_broadcast(P)).then_inc(g_in, 16)
                load_w(l, FFRQ)
                q.wait_ge(tr_free, l * N_TR + 2 * NT + CR)
                q.dma_start(rtab, tables[:, 140:1164]).then_inc(rtab_in, 16)
                for i in range(2):
                    spread(l, PJ["mk"] + i, mkst, True, 2 * i, 0, N_MEM)
                load_w(l, RKRV)
                load_w(l, RZ)
                load_w(l, MQ)
                load_w(l, MZ)
                for i in range(4):
                    spread(l, PJ["mq"] + i, mqst, False, 2 * (i // 2), 512 * (i % 2), 512)
                load_w(l, FQ)
                load_w(l, FK)
                for i in range(8):
                    spread(l, PJ["fq"] + i, qst, False, 2 * (i // 2), 512 * (i % 2), 512)
                load_w(l, FV)
                q.wait_ge(crow_ok, l + 1)
                q.dma_start(cdram, crow).then_inc(c_out, 16)
                q.wait_ge(c_out, l * 16 + 16)
                for h in range(2):
                    q.dma_start(cb[:, h, :], cdram[h].partition_broadcast(P)).then_inc(cb_in[h], 16)
                for i in range(8):
                    spread(l, PJ["fk"] + i, kst, True, 2 * (i // 2), 512 * (i % 2), 512)
                load_w(l, FZ)
                load_w(l, WO0)
                for h in range(2, FOX):
                    q.wait_ge(s_free, l * N_IT + N_MI + NT * (h - 1) + CR)
                    q.dma_start(cb[:, h % 2, :], cdram[h].partition_broadcast(P)).then_inc(cb_in[h % 2], 16)
                q.wait_ge(s_free, l * N_IT + N_IT + CR)
                q.dma_start(gpost, g_post[l].partition_broadcast(P)).then_inc(gp_in, 16)
                load_w(l, WO1)
                q.wait_ge(pj_free, l * N_PJ + PJ["wo0"] + CR)
                for i in range(2):
                    q.wait_ge(st_out[i], l * 16 * (NT // 2) + 16)
                for s in range(2):
                    q.dma_start(tp[:, s, :], out_rows[s]).then_inc(xr_in[s], 16)
                for s in range(NT):
                    q.wait_ge(out_ok, l * NT + s + 1 + CR)
                    q.dma_start(out_rows[s], xin[:, s, :]).then_inc(st_out[s % 2], 16)
                    if s + 2 < NT:
                        q.dma_start(tp[:, s % 2, :], out_rows[s + 2]).then_inc(xr_in[s % 2], 16)
            for i in range(2):
                q.wait_ge(st_out[i], 16 + DEPTH * 16 * (NT // 2))
            q.wait_ge(c_out, 16 * DEPTH)

        @block.gpsimd
        def _(pool):
            pool.memset(negh[:], -0.5)
            pool.memset(msk[:], 0.0)
            pool.drain()
            pool.affine_select(out=ident_b, in_=ident_b, compare_op=ALU.not_equal, fill=1.0, base=0,
                               pattern=[[-1, P]], channel_multiplier=1)
            pool.affine_select(out=mask_b, in_=mask_b, compare_op=ALU.is_ge, fill=-1e30, base=0,
                               pattern=[[-1, P]], channel_multiplier=1)
            pool.drain()
            pool.memset(ones1[:], 1.0)
            pool.memset(gcol[:, G_ONE, :], 1.0).then_inc(consts, 1)

            def chunk_max(l, c):
                pool.wait_ge(amax_p, l * NCH + c + 1)
                pool.sem_inc(held, 1)
                pool.partition_all_reduce(amax[:], pmax[:], P, RMAX).then_inc(amax_a, 1)

            def inv_rms(l, j):
                pool.wait_ge(ss_ok, l * N_SS + j + 1)
                pool.sem_inc(held, 1)
                pool.tensor_scalar(msq[:, j:j + 1], ssq[:, j:j + 1], 1.0 / D, EPS, ALU.mult, ALU.add)
                pool.drain()
                pool.tensor_tensor(rstd[:, j:j + 1], msq[:, j:j + 1], negh[:, 0:1], ALU.pow).then_inc(rstd_ok, 1)

            pool.wait_ge(consts, 1)
            with pool.Fori(0, DEPTH) as l:
                for j in range(NMT + NT):
                    inv_rms(l, j)
                    if j == 3:
                        chunk_max(l, MKV)
                chunk_max(l, FFRQ)
                chunk_max(l, RKRV)
                chunk_max(l, RZ)
                for s in range(NT):
                    pool.wait_ge(gss_ok, l * NT + s + 1)
                    pool.sem_inc(held, 1)
                    pool.tensor_scalar(gms[:, s, :], gss[:, s, :], 1.0 / HD, EPS, ALU.mult, ALU.add)
                    pool.drain()
                    pool.tensor_tensor(gnr[:, s, :], gms[:, s, :], negh[:], ALU.pow).then_inc(gnr_ok, 1)
                for c in range(MQ, NCH):
                    chunk_max(l, c)
                for j in range(NMT + NT, N_SS):
                    inv_rms(l, j)

        @block.scalar
        def _(act):
            def prep(l, c, k):
                if not 3 <= k <= 6:
                    return
                width, slot = CHUNKS[c][0], c % 2
                if k == 3:
                    act.wait_ge(w_scale, l * NCH + c + 1)
                    if c >= 2:
                        act.wait_ge(pj_full, l * N_FULL + n_full(LAST[c - 2] + 1))
                for dt in (2 * (k - 3), 2 * (k - 3) + 1):
                    last = act.activation(wp[:, slot, 0, dt, 0:width], stage[:, dt, 0:width], ACT.Copy,
                                          scale=gs[:, slot, dt:dt + 1])
                last.then_inc(w_hi, 1)

            def split_hi(l, u, dst, n):
                act.wait_ge(pj_full, l * N_FULL + n_full(u) + 1)
                if u in NAT_AT and NAT_AT[u] >= 2:
                    prev = NAT[NAT_AT[u] - 2][0]
                    act.wait_ge(stk_in[NAT_AT[u] % 2], l * NAT_LAYER + nat_count(prev))
                act.activation(dst, pj[:, u % 2, 0:n], ACT.Copy).then_inc(pj_hi, 1)

            def tr_split_hi(l, u, dst, shape_t):
                act.wait_ge(tr_full, l * N_TR + u + 1)
                n = shape_t * P
                src = tr_bank(u)[:, 0:n]
                if len(dst.shape) == 3:
                    src = src.rearrange("p (t n) -> p t n", t=shape_t)
                act.activation(dst, src, ACT.Copy).then_inc(tr_hi, 1)

            def silu(l, u, c, width):
                act.wait_ge(pj_full, l * N_FULL + n_full(u) + 1)
                act.activation(tp[:, u % 2, 0:width], pj[:, u % 2, 0:width], ACT.Silu,
                               scale=unsc[:, c:c + 1]).then_inc(silu_ok, 1)

            def attend(l, i0, n_items):
                for i in range(i0, i0 + n_items + 1):
                    if i < i0 + n_items:
                        kind, h, t, nk = ITEMS[i]
                        act.wait_ge(nm_ok, l * N_IT + i + 1)
                        act.activation(tp[:, i % 3, 0:nk * P], tp[:, i % 3, 0:nk * P], ACT.Exp,
                                       bias=nm[:, i % 4:i % 4 + 1], scale=sc2[:, kind, 0:1],
                                       accum_out=rs[:, h % 2, t:t + 1]).then_inc(p_ok, 1)
                    if i > i0:
                        j = i - 1
                        nk = ITEMS[j][3]
                        if j - 2 >= i0:
                            act.wait_ge(pv_done, l * N_IT + j - 1)
                        for b, u in enumerate(ITEM_TR[j]):
                            w = min(4, nk - 4 * b)
                            tr_split_hi(l, u, pt[:, j % 2, 0, 512 * b:512 * b + w * P], w)

            act.wait_ge(tab_in, 16)
            with act.Fori(0, DEPTH) as l:
                def squares(j):
                    if j < NT:
                        act.wait_ge(x_in[j], 16)
                        if j == 0:
                            act.wait_ge(out_ok, l * NT + CR)
                    elif j == NT:
                        act.wait_ge(mem_in, l * 16 + 16)
                    if j >= 1:
                        act.wait_ge(ss_ok, l * N_SS + j)
                    act.activation(junk, norm_rows(j), ACT.Square, accum_out=ssq[:, j:j + 1]).then_inc(ss_ok, 1)

                squares(0)
                squares(1)
                for j in range(NT + NMT):
                    if j + 2 < NT + NMT:
                        squares(j + 2)
                    dst, cs = norm_dst(j)
                    for b in range(2):
                        tr_split_hi(l, TR_NORM + 2 * j + b, dst[:, 0, 4 * b:4 * b + 4, cs], 4)
                    if j >= 1:
                        prep(l, MKV, j - 1)
                for i in range(4):
                    u = i
                    if i < 2:
                        split_hi(l, u, pt[:, NAT_AT[u] % 2, 0, 0:N_MEM], N_MEM)
                    else:
                        split_hi(l, u, mvs[:, 0, i - 2, :], MEM_W)
                    prep(l, FFRQ, 2 * i)
                    prep(l, FFRQ, 2 * i + 1)
                for k in range(NT):
                    prep(l, RKRV, k)
                for k in range(NT):
                    prep(l, RZ, k)
                act.wait_ge(fa_ok, l + 1)
                act.activation(fabs[:], fabs[:], ACT.Exp, scale=-1.0).then_inc(fe_ok, 1)
                act.wait_ge(fe_ok, l + 1)
                act.activation(fabs[:], fabs[:], ACT.Ln, bias=1.0).then_inc(fl_ok, 1)
                for s in range(NT):
                    silu(l, PJ["rz"] + s, RZ, RET_W)
                    prep(l, MQ, s)
                for i in range(4):
                    u = PJ["mq"] + i
                    split_hi(l, u, pt[:, NAT_AT[u] % 2, 0, 0:512], 512)
                    prep(l, MZ, 2 * i)
                    prep(l, MZ, 2 * i + 1)
                attend(l, 0, N_MI)
                for s in range(NT):
                    silu(l, PJ["mz"] + s, MZ, MEM_W)
                    prep(l, FQ, s)
                for i in range(8):
                    u = PJ["fq"] + i
                    split_hi(l, u, pt[:, NAT_AT[u] % 2, 0, 0:512], 512)
                    prep(l, FK, i)
                for i in range(8):
                    u = PJ["fk"] + i
                    split_hi(l, u, pt[:, NAT_AT[u] % 2, 0, 0:512], 512)
                    prep(l, FV, i)
                for s in range(NT):
                    split_hi(l, PJ["fv"] + s, fvs[:, 0, s, :], FOX_W)
                    prep(l, FZ, s)
                attend(l, N_MI, N_IT - N_MI)
                for s in range(NT + 1):
                    if s < NT:
                        silu(l, PJ["fz"] + s, FZ, FOX_W)
                        prep(l, WO0, s)
                    if s >= 1:
                        for b in range(2):
                            tr_split_hi(l, TR_Y + 2 * (s - 1) + b, hT[:, 0, 4 * b:4 * b + 4, (s - 1) * P:s * P], 4)
                for s in range(NT):
                    prep(l, WO1, s)
                for s in range(NT):
                    j = NMT + NT + s
                    act.wait_ge(o_ok, l * NT + s + 1)
                    act.wait_ge(ss_ok, l * N_SS + j)
                    act.activation(words(8192, 1024), ost[:, s, :], ACT.Square,
                                   accum_out=ssq[:, j:j + 1]).then_inc(ss_ok, 1)

        @block.tensor
        def _(pe):
            def open_unit(l, u):
                after_o = u - 1 in range(PJ["mo"], PJ["mo"] + MEM) or u - 1 in range(PJ["fo"], PJ["fo"] + FOX)
                pe.wait_ge(pj_free, l * N_PJ + u + (2 if after_o else 1))

            def rows_unit(l, u, c, lhs, t, c0, n, tiles=(0, ND)):
                if tiles[0] == 0:
                    open_unit(l, u)
                for dt in range(*tiles):
                    for a, b in ((0, 0), (0, 1), (1, 0)):
                        last = pe.matmul(pj[:, u % 2, 0:n], lhs[:, a, dt, t * P:t * P + P],
                                         wp[:, c % 2, b, dt, c0:c0 + n],
                                         start=(dt == 0 and a + b == 0), stop=(dt == ND - 1 and a == 1))
                if tiles[1] == ND:
                    last.then_inc(pj_full, 1)

            def cols_unit(l, u, c, rhs, e0, s0, n):
                open_unit(l, u)
                for dt in range(ND):
                    for a, b in ((0, 0), (0, 1), (1, 0)):
                        last = pe.matmul(pj[:, u % 2, 0:n], wp[:, c % 2, a, dt, e0:e0 + P],
                                         rhs[:, b, dt, s0:s0 + n],
                                         start=(dt == 0 and a + b == 0), stop=(dt == ND - 1 and a == 1))
                last.then_inc(pj_full, 1)

            def chunk_ready(l, c):
                pe.wait_ge(w_ok, l * NCH + c + 2)

            def transposes(l, u, srcs, rows=P):
                pe.wait_ge(tr_free, l * N_TR + u + (0 if TR_ATT <= u < TR_Y else 1))
                if rows != P:
                    pe.sem_inc(held, 1)
                for k, src in enumerate(srcs):
                    last = pe.transpose(tr_bank(u)[0:rows, k * P:k * P + P], src, ident)
                last.then_inc(tr_full, 1)

            def ret_out(l, s):
                pe.wait_ge(ra_ok, l * NT + s + 1)
                if s > 0:
                    pe.wait_ge(state_ok, l * NT + s)
                    pe.wait_ge(ro_free, l * NT + s)
                r = s % 2
                for h in range(RET):
                    e = slice(h * HD, h * HD + HD)
                    last = pe.matmul(ret_o[:, e], aT[:, r, h * P:h * P + P], rv[:, r, e], start=True, stop=True)
                if s > 0:
                    for h in range(RET):
                        e = slice(h * HD, h * HD + HD)
                        last = pe.matmul(ret_o[:, 256 + h * HD:256 + h * HD + HD], qkT[:, r, 0, h * P:h * P + P],
                                         state[:, r, e], start=True, stop=True)
                last.then_inc(ro_full, 1)

            def ret_transposes(l, s):
                pe.wait_ge(kr_ok, l * NT + s + 1)
                transposes(l, TR_RET + 2 * s, [qr[:, s, h * HD:h * HD + HD] for h in range(RET)], HD)
                transposes(l, TR_RET + 2 * s + 1, [kr[:, s % 2, h * HD:h * HD + HD] for h in range(RET)], HD)

            def ret_scores(l, s):
                r = s % 2
                pe.wait_ge(tr_free, l * N_TR + TR_RET + 2 * s + 2 + CR)
                for h in range(RET):
                    last = pe.matmul(ret_a[:, h * P:h * P + P], qkT[:, r, 1, h * P:h * P + P],
                                     qkT[:, r, 0, h * P:h * P + P], start=True, stop=True)
                last.then_inc(ra_full, 1)
                if s > 0:
                    pe.wait_ge(state_ok, l * NT + s)
                for h in range(RET):
                    e = slice(h * HD, h * HD + HD)
                    last = pe.matmul(ret_kv[:, e], kz[:, r, e], rv[:, r, e], start=True, stop=True)
                last.then_inc(rkv_full, 1)

            def item_scores(l, i):
                kind, h, t, nk = ITEMS[i]
                pe.wait_ge(s_free, l * N_IT + i + 1)
                q = (qst if kind else mqst)[:, h, t * P:t * P + P]
                k = kst if kind else mkst
                for a in range(0, nk * P, 512):
                    n = min(512, nk * P - a)
                    o = sp[:, i % 2, a:a + n]
                    diag = kind and a + n == nk * P
                    pe.matmul(o, q, k[:, h, 0, a:a + n], start=True, stop=False)
                    last = pe.matmul(o, q, k[:, h, 1, a:a + n], start=False, stop=not diag)
                    if diag:
                        last = pe.matmul(sp[:, i % 2, a + n - P:a + n], ident_b, mask_b, start=False, stop=True)
                last.then_inc(s_full, 1)

            def item_transposes(l, i):
                pe.wait_ge(p_ok, l * N_IT + i + 1)
                nk = ITEMS[i][3]
                for b, u in enumerate(ITEM_TR[i]):
                    transposes(l, u, [tp[:, i % 3, k * P:k * P + P] for k in range(4 * b, min(nk, 4 * b + 4))])

            def item_values(l, i):
                kind, h, t, nk = ITEMS[i]
                u = (PJ["fo"] if kind else PJ["mo"]) + h
                if t == 0:
                    open_unit(l, u)
                pe.wait_ge(tr_free, l * N_TR + ITEM_TR[i][-1] + 1 + CR)
                v = fvs if kind else mvs
                o = pj[:, 0, t * HD:t * HD + HD]
                e = slice(h * HD, h * HD + HD)
                for k in range(nk):
                    for a, b in ((0, 0), (0, 1), (1, 0)):
                        last = pe.matmul(o, pt[:, i % 2, a, k * P:k * P + P], v[:, b, k, e],
                                         start=(k == 0 and a + b == 0), stop=(k == nk - 1 and a == 1))
                last.then_inc(pv_done, 1)

            def attend(l, i0, n_items):
                end = i0 + n_items
                pe.wait_ge(pj_free, l * N_PJ + PJ["fo" if ITEMS[i0][0] else "mo"] + CR)
                pe.wait_ge(tr_free, l * N_TR + ITEM_TR[i0][0] + CR)
                item_scores(l, i0)
                item_scores(l, i0 + 1)
                for i in range(i0, end + 2):
                    if i + 2 < end:
                        item_scores(l, i + 2)
                    if i0 <= i - 2:
                        item_values(l, i - 2)
                    if i < end:
                        item_transposes(l, i)

            pe.wait_ge(consts, 1)
            pe.wait_ge(tab_in, 16)
            with pe.Fori(0, DEPTH) as l:
                for j in range(NMT + NT):
                    pe.wait_ge(xh_ok, l * (NMT + NT) + j + 1)
                    for b in range(2):
                        transposes(l, TR_NORM + 2 * j + b,
                                   [norm_rows(j)[:, k:D:ND] for k in range(4 * b, 4 * b + 4)])
                pe.wait_ge(tr_free, l * N_TR + TR_RET + CR)
                chunk_ready(l, MKV)
                for i in range(2):
                    cols_unit(l, PJ["mk"] + i, MKV, memT, i * P, 0, N_MEM)
                for i in range(NMT):
                    rows_unit(l, PJ["mv"] + i, MKV, memT, i, MEM_W, MEM_W)
                chunk_ready(l, FFRQ)
                for s in range(NT):
                    rows_unit(l, PJ["ffrq"] + s, FFRQ, hT, s, 0, FOX + RET_W)
                chunk_ready(l, RKRV)
                for s in range(NT + 2):
                    if s < NT:
                        rows_unit(l, PJ["rkrv"] + s, RKRV, hT, s, 0, 2 * RET_W, (0, ND // 2))
                    if 1 <= s <= NT:
                        ret_transposes(l, s - 1)
                    if s >= 2:
                        ret_out(l, s - 2)
                    if s < NT:
                        rows_unit(l, PJ["rkrv"] + s, RKRV, hT, s, 0, 2 * RET_W, (ND // 2, ND))
                    if 1 <= s <= NT:
                        ret_scores(l, s - 1)
                pe.wait_ge(lf_ok, l + 1)
                for b in range(2):
                    transposes(l, TR_F + b, [fcol[:, s, :] for s in range(4 * b, 4 * b + 4)], FOX)
                chunk_ready(l, RZ)
                for s in range(NT):
                    rows_unit(l, PJ["rz"] + s, RZ, hT, s, 0, RET_W)
                chunk_ready(l, MQ)
                for i in range(4):
                    cols_unit(l, PJ["mq"] + i, MQ, hT, (i // 2) * P, 512 * (i % 2), 512)
                for b in range(2):
                    pe.wait_ge(stk_in[b], l * NAT_LAYER + nat_count(PJ["mq"] + 2 + (b - NAT_AT[PJ["mq"] + 2]) % 2))
                attend(l, 0, N_MI)
                chunk_ready(l, MZ)
                for s in range(NT):
                    rows_unit(l, PJ["mz"] + s, MZ, hT, s, 0, MEM_W)
                chunk_ready(l, FQ)
                for i in range(8):
                    cols_unit(l, PJ["fq"] + i, FQ, hT, (i // 2) * P, 512 * (i % 2), 512)
                chunk_ready(l, FK)
                for i in range(8):
                    cols_unit(l, PJ["fk"] + i, FK, hT, (i // 2) * P, 512 * (i % 2), 512)
                chunk_ready(l, FV)
                for s in range(NT):
                    rows_unit(l, PJ["fv"] + s, FV, hT, s, 0, FOX_W)
                for b in range(2):
                    pe.wait_ge(stk_in[b], l * NAT_LAYER + NAT_LAYER)
                attend(l, N_MI, N_IT - N_MI)
                chunk_ready(l, FZ)
                for s in range(NT + 1):
                    if s < NT:
                        rows_unit(l, PJ["fz"] + s, FZ, hT, s, 0, FOX_W)
                    if s >= 1:
                        pe.wait_ge(ys_ok, l * NT + s)
                        for b in range(2):
                            transposes(l, TR_Y + 2 * (s - 1) + b,
                                       [y[:, s - 1, k:D:ND] for k in range(4 * b, 4 * b + 4)])
                chunk_ready(l, WO0)
                pe.wait_ge(tr_free, l * N_TR + N_TR + CR)
                for s in range(NT):
                    rows_unit(l, PJ["wo0"] + s, WO0, hT, s, 0, 512)
                chunk_ready(l, WO1)
                for s in range(NT):
                    rows_unit(l, PJ["wo1"] + s, WO1, hT, s, 0, 512)

        @block.vector
        def _(dve):
            def prep(l, c, k):
                width, _, g = CHUNKS[c]
                slot = c % 2
                if k < 2:
                    if k == 0:
                        dve.wait_ge(w_in_sb, l * 16 * NCH + 16 * c + 16)
                    dve.tensor_reduce(rmax[:, 4 * k:4 * k + 4], stage[:, 4 * k:4 * k + 4, 0:width], AX.X, ALU.max,
                                      apply_absolute_value=True)
                if k == 1:
                    dve.drain()
                    dve.tensor_tensor(rmax[:], rmax[:], gabs[:, g, :], ALU.mult)
                    dve.drain()
                    dve.tensor_reduce(pmax[:], rmax[:], AX.X, ALU.max).then_inc(amax_p, 1)
                if k == 2:
                    dve.wait_ge(amax_a, l * NCH + c + 1)
                    dve.tensor_scalar(amax[:], amax[:], 2.0 ** -30, None, ALU.max)
                    dve.drain()
                    power_of_two(sval[:, c:c + 1], unsc[:, c:c + 1], amax[:])
                    dve.tensor_scalar(gs[:, slot, :], gcol[:, g, :], sval[:, c:c + 1], None,
                                      ALU.mult).then_inc(w_scale, 1)
                if 3 <= k <= 6:
                    if k == 3:
                        dve.drain()
                    dve.wait_ge(w_hi, l * 4 * NCH + 4 * c + k - 2)
                    for dt in (2 * (k - 3), 2 * (k - 3) + 1):
                        last = dve.scalar_tensor_tensor(wp[:, slot, 1, dt, 0:width], stage[:, dt, 0:width],
                                                        gs[:, slot, dt:dt + 1], wp[:, slot, 0, dt, 0:width],
                                                        ALU.mult, ALU.subtract)
                    if k == 6:
                        last.then_inc(w_ok, 1)

            def power_of_two(up, down, m):
                dve.tensor_scalar(down.bitcast(I32), m.bitcast(I32), 0x7F800000, None, ALU.bitwise_and)
                dve.drain()
                dve.tensor_scalar(up.bitcast(I32), down.bitcast(I32), -1.0, float(0x7F000000), ALU.mult, ALU.add)
                dve.drain()

            def split_lo(l, u, hi, lo, n):
                dve.wait_ge(pj_hi, l * N_SPLIT + SPLIT.index(u) + 1)
                dve.tensor_tensor(lo, pj[:, u % 2, 0:n], hi, ALU.subtract).then_inc(pj_free, 1)

            def tr_split_lo(l, u, hi, lo, w):
                dve.wait_ge(tr_hi, l * N_HI + n_hi(u) + 1)
                src = tr_bank(u)[:, 0:w * P]
                if len(hi.shape) == 3:
                    src = src.rearrange("p (t n) -> p t n", t=w)
                dve.tensor_tensor(lo, src, hi, ALU.subtract).then_inc(tr_free, 1)

            def gate(l, u, z, s, c0, width):
                dve.wait_ge(silu_ok, l * N_Z + z + 1)
                yv = y[:, s, c0:c0 + width]
                dve.tensor_tensor(yv, yv, tp[:, u % 2, 0:width], ALU.mult).then_inc(pj_free, 1)

            def rotary(src, dst, scale):
                s8 = src.rearrange("p (h j) -> p h j", j=32)
                dve.scalar_tensor_tensor(rot[:, 0, :].rearrange("p (h j) -> p h j", j=32), s8, scale, cos_now,
                                         ALU.mult, ALU.mult)
                last = dve.scalar_tensor_tensor(rot[:, 1, :].rearrange("p (h j) -> p h j", j=32), s8, scale, sin_now,
                                                ALU.mult, ALU.mult)
                return last

            def rotary_sum(dst):
                t1 = rot[:, 0, :].rearrange("p (h two j) -> p h two j", two=2, j=32)
                t2 = rot[:, 1, :].rearrange("p (h two j) -> p h two j", two=2, j=32)
                d = dst.rearrange("p (h two j) -> p h two j", two=2, j=32)
                dve.tensor_tensor(d[:, :, 0, :], t1[:, :, 0, :], t2[:, :, 1, :], ALU.subtract)
                return dve.tensor_tensor(d[:, :, 1, :], t1[:, :, 1, :], t2[:, :, 0, :], ALU.add)

            def heads(ap):
                return ap.rearrange("p (h e) -> p h e", h=RET)

            def over_head(col, n=P):
                return col.unsqueeze(2).to_broadcast([n, RET, HD])

            def item_max(l, i, i0):
                kind, h, t, nk = ITEMS[i]
                n = nk * P
                dve.wait_ge(s_full, l * N_IT + i + 1)
                if i - 3 >= i0:
                    dve.wait_ge(tr_full, l * N_TR + ITEM_TR[i - 3][-1] + 1)
                if kind and t == 0:
                    dve.wait_ge(cb_in[h % 2], l * 16 * (FOX // 2) + 16 * (h // 2) + 16)
                dve.sem_inc(held, 1)
                bias = cb[:, h % 2, 0:n] if kind else mzero
                dve.tensor_tensor_reduce(tp[:, i % 3, 0:n], sp[:, i % 2, 0:n], bias, 1.0, -3.0e38, ALU.add, ALU.max,
                                         mx[:, i % 4:i % 4 + 1]).then_inc(s_free, 1)
                dve.drain()
                dve.tensor_scalar(nm[:, i % 4:i % 4 + 1], mx[:, i % 4:i % 4 + 1], sc2[:, kind, 1:2], None,
                                  ALU.mult).then_inc(nm_ok, 1)

            def head_out(l, i):
                kind, h, t, nk = ITEMS[i]
                u = (PJ["fo"] if kind else PJ["mo"]) + h
                c = FV if kind else MKV
                c0 = (0 if kind else FOX_W + RET_W) + h * HD
                r = h % 2
                dve.wait_ge(pv_done, l * N_IT + i + 1)
                dve.reciprocal(rec[:, r, :], rs[:, r, :])
                dve.drain()
                dve.tensor_scalar(rec[:, r, :], rec[:, r, :], unsc[:, c:c + 1], None, ALU.mult)
                dve.drain()
                dve.tensor_tensor(y[:, :, c0:c0 + HD], pj[:, 0, :].rearrange("p (t e) -> p t e", t=NT),
                                  rec[:, r, :].unsqueeze(2).to_broadcast([P, NT, HD]), ALU.mult).then_inc(pj_free, 1)

            def attend(l, i0, n_items):
                end = i0 + n_items
                item_max(l, i0, i0)
                item_max(l, i0 + 1, i0)
                for i in range(i0, end + 2):
                    j = i - 1
                    if i0 <= j < end:
                        nk = ITEMS[j][3]
                        for b, u in enumerate(ITEM_TR[j]):
                            w = min(4, nk - 4 * b)
                            sl = slice(512 * b, 512 * b + w * P)
                            tr_split_lo(l, u, pt[:, j % 2, 0, sl], pt[:, j % 2, 1, sl], w)
                    if i + 2 < end:
                        item_max(l, i + 2, i0)
                    if i0 <= i - 2 and ITEMS[i - 2][2] == NT - 1:
                        head_out(l, i - 2)
                dve.drain()

            def attention_scale(kind, cq, ck):
                dve.tensor_scalar(sc2[:, kind, 0:1], unsc[:, cq:cq + 1], unsc[:, ck:ck + 1], HD ** -0.5,
                                  ALU.mult, ALU.mult)
                dve.tensor_scalar(sc2[:, kind, 2:3], sval[:, cq:cq + 1], sval[:, ck:ck + 1], -(HD ** 0.5),
                                  ALU.mult, ALU.mult)
                dve.drain()
                dve.tensor_scalar(sc2[:, kind, 1:2], sc2[:, kind, 0:1], -1.0, None, ALU.mult)
                dve.drain()

            dve.wait_ge(consts, 1)
            dve.sem_inc(pj_free, CR)
            dve.sem_inc(tr_free, CR)
            dve.sem_inc(s_free, CR)
            dve.sem_inc(w_ok, 1)
            dve.sem_inc(out_ok, CR)
            dve.wait_ge(tab_in, 16)
            with dve.Fori(0, DEPTH) as l:
                dve.wait_ge(g_in, l * 48 + 48)
                dve.scalar_tensor_tensor(gabs[:], gcol[:], -1.0, gcol[:], ALU.mult, ALU.max).then_inc(gabs_ok, 1)
                for j in range(-1, NT + NMT):
                    if j + 1 < NT + NMT:
                        dve.wait_ge(rstd_ok, l * N_SS + j + 2)
                        dve.tensor_scalar(norm_rows(j + 1), norm_rows(j + 1), rstd[:, j + 1:j + 2], None,
                                          ALU.mult).then_inc(xh_ok, 1)
                    if j >= 0:
                        dst, cs = norm_dst(j)
                        for b in range(2):
                            tr_split_lo(l, TR_NORM + 2 * j + b, dst[:, 0, 4 * b:4 * b + 4, cs],
                                        dst[:, 1, 4 * b:4 * b + 4, cs], 4)
                    if j >= 1:
                        prep(l, MKV, j - 1)
                for i in range(4):
                    if i < 2:
                        sl = NAT_AT[i] % 2
                        split_lo(l, i, pt[:, sl, 0, 0:N_MEM], pt[:, sl, 1, 0:N_MEM], N_MEM)
                    else:
                        split_lo(l, i, mvs[:, 0, i - 2, :], mvs[:, 1, i - 2, :], MEM_W)
                    prep(l, FFRQ, 2 * i)
                    prep(l, FFRQ, 2 * i + 1)
                dve.wait_ge(rtab_in, l * 16 + 16)
                dve.sem_inc(held, 1)
                for s in range(NT):
                    u = PJ["ffrq"] + s
                    dve.drain()
                    dve.wait_ge(pj_full, l * N_FULL + n_full(u) + 1)
                    cos_now = cos_t[:, 32 * s:32 * s + 32].unsqueeze(1).to_broadcast([P, 2 * RET, 32])
                    sin_now = sin_t[:, 32 * s:32 * s + 32].unsqueeze(1).to_broadcast([P, 2 * RET, 32])
                    dve.scalar_tensor_tensor(fcol[:, s, :], pj[:, u % 2, 0:FOX], unsc[:, FFRQ:FFRQ + 1], bfb[:],
                                             ALU.mult, ALU.add)
                    rotary(pj[:, u % 2, FOX:FOX + RET_W], None, unsc[:, FFRQ:FFRQ + 1]).then_inc(pj_free, 1)
                    dve.drain()
                    rotary_sum(qr[:, s, :])
                    prep(l, RKRV, s)
                dve.drain()
                dve.scalar_tensor_tensor(fabs[:], fcol[:], -1.0, fcol[:], ALU.mult, ALU.max).then_inc(fa_ok, 1)
                dve.tensor_scalar(sc2[:, 0, 0:1], unsc[:, RKRV:RKRV + 1], HD ** -0.5, None, ALU.mult)
                dve.drain()
                for s in range(NT + 3):
                    if 1 <= s <= NT:
                        n = s - 1
                        r = n % 2
                        for b in range(2):
                            u = TR_RET + 2 * n + b
                            dve.wait_ge(tr_full, l * N_TR + u + 1)
                            dve.tensor_copy(qkT[:, r, b, :], tr[0:HD, u % 2, :]).then_inc(tr_free, 1)
                    if 2 <= s < NT + 2:
                        n = s - 2
                        r = n % 2
                        dve.wait_ge(ro_full, l * NT + n + 1)
                        if n == 0:
                            dve.tensor_copy(ro[:, r, :], ret_o[:, 0:256]).then_inc(ro_free, 1)
                        else:
                            dve.tensor_tensor(heads(rcr), heads(ret_o[:, 256:512]), over_head(xi_c), ALU.mult)
                            dve.drain()
                            dve.tensor_tensor(ro[:, r, :], ret_o[:, 0:256], rcr, ALU.add).then_inc(ro_free, 1)
                        dve.drain()
                        dve.tensor_tensor(rsq, ro[:, r, :], ro[:, r, :], ALU.mult)
                        dve.drain()
                        dve.tensor_reduce(gss[:, n, :], heads(rsq), AX.X, ALU.add).then_inc(gss_ok, 1)
                    if s < NT:
                        u = PJ["rkrv"] + s
                        r = s % 2
                        dve.drain()
                        dve.wait_ge(pj_full, l * N_FULL + n_full(u) + 1)
                        cos_now = cos_t[:, 32 * s:32 * s + 32].unsqueeze(1).to_broadcast([P, 2 * RET, 32])
                        sin_now = sin_t[:, 32 * s:32 * s + 32].unsqueeze(1).to_broadcast([P, 2 * RET, 32])
                        rotary(pj[:, u % 2, 0:RET_W], None, sc2[:, 0, 0:1])
                        dve.tensor_scalar(rv[:, r, :], pj[:, u % 2, RET_W:2 * RET_W], unsc[:, RKRV:RKRV + 1], None,
                                          ALU.mult).then_inc(pj_free, 1)
                        dve.drain()
                        rotary_sum(kr[:, r, :])
                        dve.drain()
                        dve.tensor_tensor(heads(kz[:, r, :]), heads(kr[:, r, :]), over_head(zeta_c),
                                          ALU.mult).then_inc(kr_ok, 1)
                    if s >= 3:
                        n = s - 3
                        dve.wait_ge(gnr_ok, l * NT + n + 1)
                        dve.tensor_tensor(heads(y[:, n, FOX_W:FOX_W + RET_W]), heads(ro[:, n % 2, :]),
                                          over_head(gnr[:, n, :]), ALU.mult)
                    if 1 <= s <= NT:
                        n = s - 1
                        r = n % 2
                        dve.wait_ge(ra_full, l * NT + n + 1)
                        dve.tensor_tensor(aT[:, r, :], ret_a, decay_t, ALU.mult).then_inc(ra_ok, 1)
                        dve.wait_ge(rkv_full, l * NT + n + 1)
                        if n == 0:
                            dve.tensor_copy(state[:, 1, :], ret_kv).then_inc(state_ok, 1)
                        else:
                            dve.tensor_tensor(heads(rst), heads(state[:, r, :]), over_head(dc_c[0:HD, :], HD),
                                              ALU.mult)
                            dve.drain()
                            dve.tensor_tensor(state[:, 1 - r, :], rst, ret_kv, ALU.add).then_inc(state_ok, 1)
                    if s < NT:
                        prep(l, RZ, s)
                dve.wait_ge(fl_ok, l + 1)
                dve.scalar_tensor_tensor(fcol[:], fcol[:], 0.0, fabs[:], ALU.min, ALU.subtract).then_inc(lf_ok, 1)
                for b in range(2):
                    u = TR_F + b
                    dve.wait_ge(tr_full, l * N_TR + u + 1)
                    dve.tensor_tensor_scan(crow[:, 512 * b:512 * b + 512],
                                           ones1[0:FOX, :].to_broadcast([FOX, 512]), tr[0:FOX, u % 2, :],
                                           crow[:, 511:512] if b else 0.0, ALU.mult, ALU.add).then_inc(tr_free, 1)
                    dve.drain()
                for s in range(NT):
                    gate(l, PJ["rz"] + s, s, s, FOX_W, RET_W)
                    prep(l, MQ, s)
                for i in range(4):
                    sl = NAT_AT[PJ["mq"] + i] % 2
                    split_lo(l, PJ["mq"] + i, pt[:, sl, 0, 0:512], pt[:, sl, 1, 0:512], 512)
                    prep(l, MZ, 2 * i)
                    prep(l, MZ, 2 * i + 1)
                attention_scale(0, MQ, MKV)
                dve.memset(mzero, 0.0)
                dve.drain()
                attend(l, 0, N_MI)
                for s in range(NT):
                    gate(l, PJ["mz"] + s, NT + s, s, FOX_W + RET_W, MEM_W)
                    prep(l, FQ, s)
                for i in range(8):
                    sl = NAT_AT[PJ["fq"] + i] % 2
                    split_lo(l, PJ["fq"] + i, pt[:, sl, 0, 0:512], pt[:, sl, 1, 0:512], 512)
                    prep(l, FK, i)
                attention_scale(1, FQ, FK)
                dve.tensor_scalar(crow, crow, sc2[0:FOX, 1, 2:3], None, ALU.mult).then_inc(crow_ok, 1)
                for i in range(8):
                    sl = NAT_AT[PJ["fk"] + i] % 2
                    split_lo(l, PJ["fk"] + i, pt[:, sl, 0, 0:512], pt[:, sl, 1, 0:512], 512)
                    prep(l, FV, i)
                for s in range(NT):
                    split_lo(l, PJ["fv"] + s, fvs[:, 0, s, :], fvs[:, 1, s, :], 512)
                    prep(l, FZ, s)
                attend(l, N_MI, N_IT - N_MI)
                for s in range(NT + 1):
                    if s < NT:
                        gate(l, PJ["fz"] + s, 2 * NT + s, s, 0, FOX_W)
                        dve.drain()
                        one = slice(s, s + 1)
                        dve.tensor_reduce(ymax[:, one], y[:, s, :], AX.X, ALU.max, apply_absolute_value=True)
                        dve.drain()
                        dve.tensor_scalar(ymax[:, one], ymax[:, one], 2.0 ** -30, None, ALU.max)
                        dve.drain()
                        power_of_two(ysc[:, one], yun[:, one], ymax[:, one])
                        dve.tensor_scalar(y[:, s, :], y[:, s, :], ysc[:, one], None, ALU.mult).then_inc(ys_ok, 1)
                        prep(l, WO0, s)
                    if s >= 1:
                        for b in range(2):
                            cs = slice((s - 1) * P, s * P)
                            tr_split_lo(l, TR_Y + 2 * (s - 1) + b, hT[:, 0, 4 * b:4 * b + 4, cs],
                                        hT[:, 1, 4 * b:4 * b + 4, cs], 4)
                dve.tensor_scalar(fo[:, 0, :], yun[:], unsc[:, WO0:WO0 + 1], None, ALU.mult)
                dve.drain()
                for s in range(NT):
                    u = PJ["wo0"] + s
                    dve.wait_ge(pj_full, l * N_FULL + n_full(u) + 1)
                    dve.tensor_scalar(ost[:, s, 0:512], pj[:, u % 2, :], fo[:, 0, s:s + 1], None,
                                      ALU.mult).then_inc(pj_free, 1)
                    prep(l, WO1, s)
                dve.tensor_scalar(fo[:, 1, :], yun[:], unsc[:, WO1:WO1 + 1], None, ALU.mult)
                dve.drain()
                dve.wait_ge(gp_in, l * 16 + 16)
                for s in range(NT + 1):
                    if s < NT:
                        u = PJ["wo1"] + s
                        dve.wait_ge(pj_full, l * N_FULL + n_full(u) + 1)
                        dve.tensor_scalar(ost[:, s, 512:1024], pj[:, u % 2, :], fo[:, 1, s:s + 1], None,
                                          ALU.mult).then_inc(pj_free, 1)
                        dve.drain().then_inc(o_ok, 1)
                    if s >= 1:
                        n = s - 1
                        j = NMT + NT + n
                        dve.wait_ge(rstd_ok, l * N_SS + j + 1)
                        dve.scalar_tensor_tensor(ost[:, n, :], ost[:, n, :], rstd[:, j:j + 1], gpost, ALU.mult,
                                                 ALU.mult)
                        dve.drain()
                        dve.wait_ge(xr_in[n % 2], l * 16 * (NT // 2) + 16 * (n // 2) + 16)
                        dve.tensor_tensor(ost[:, n, :], tp[:, n % 2, :], ost[:, n, :], ALU.add).then_inc(out_ok, 1)


LAST = {MKV: PJ["mv"] + NMT - 1, FFRQ: PJ["ffrq"] + 7, RKRV: PJ["rkrv"] + 7, RZ: PJ["rz"] + 7, MQ: PJ["mq"] + 3,
        MZ: PJ["mz"] + 7, FQ: PJ["fq"] + 7, FK: PJ["fk"] + 7, FV: PJ["fv"] + 7, FZ: PJ["fz"] + 7,
        WO0: PJ["wo0"] + 7, WO1: PJ["wo1"] + 7}


def shape_tables():
    import numpy as np
    half = HD // 2
    freqs = (np.float32(10000.0) ** (-np.arange(half, dtype=np.float32) / np.float32(half))).astype(np.float32)
    ang = np.arange(S, dtype=np.float32)[:, None] * freqs[None, :]
    to_rows = lambda a: a.reshape(NT, P, half).transpose(1, 0, 2).reshape(P, NT * half)
    lg = np.log(1.0 - 2.0 ** (-5.0 - np.arange(RET, dtype=np.float64)))
    idx = np.arange(P, dtype=np.float64)
    diff = idx[None, :] - idx[:, None]
    decay = np.where(diff >= 0, np.exp(lg[:, None, None] * np.maximum(diff, 0)), 0.0)
    zeta = np.exp(lg[None, :] * (P - 1 - idx)[:, None])
    xi = np.exp(lg[None, :] * (idx + 1)[:, None])
    dc = np.broadcast_to(np.exp(lg * P)[None, :], (P, RET))
    return np.concatenate([zeta, xi, dc, np.eye(P), to_rows(np.cos(ang)), to_rows(np.sin(ang)),
                           decay.transpose(1, 0, 2).reshape(P, RET * P)], axis=1).astype(np.float32)


_INS = ['x', 'mem', 'w_in', 'b_f', 'w_out', 'w_mem_kv', 'pre_norm', 'post_norm', 'mem_norm']


def kernel(**inputs):
    import numpy as _np
    import concourse.bacc as _bacc
    from concourse import mybir as _mybir
    from concourse.bass_utils import run_bass_kernel_spmd as _run

    nc = _bacc.Bacc("TRN2", target_bir_lowering=False, num_devices=1)
    arrays, args = {}, []
    feed = [(n, _np.ascontiguousarray(inputs[n])) for n in _INS] + [("tables", shape_tables())]
    for name, a in feed:
        arrays[f"in_{name}"] = a
        args.append(nc.dram_tensor(f"in_{name}", a.shape, _mybir.dt.from_np(a.dtype), kind="ExternalInput").ap())
    args.append(nc.dram_tensor("out_0", (1, S, D), _mybir.dt.float32, kind="ExternalOutput").ap())
    build(nc, *args)
    r = _run(nc, [arrays], core_ids=[0])
    return r.results[0]["out_0"]
```

```python
from contextlib import ExitStack

import concourse.bass as bass
from concourse import mybir

F32 = mybir.dt.float32
F16 = mybir.dt.float16
BF16 = mybir.dt.bfloat16
I32 = mybir.dt.int32
ALU = mybir.AluOpType
ACT = mybir.ActivationFunctionType
AX = mybir.AxisListType
RMAX = bass.bass_isa.ReduceOp.max

P = 128
D = 1024
S = 1024
DEPTH = 2
HD = 64
N_MEM = 256
FOX, RET, MEM = 8, 4, 4
EPS = 1e-6
ND = D // P
NT = S // P
NMT = N_MEM // P
HALF = S // 512

FOX_W, RET_W, MEM_W = FOX * HD, RET * HD, MEM * HD
C_FF = 4 * FOX_W
C_RQ = C_FF + FOX
C_RK = C_RQ + RET_W
C_RZ = C_RK + 2 * RET_W
C_MQ = C_RZ + RET_W
C_MZ = C_MQ + MEM_W

FFRQ, RKRV, RZ, MKV, MQ, MZ, FQ, FK, FV, FZ, WO0, WO1 = range(12)
G_PRE, G_MEM, G_ONE = range(3)
CHUNKS = [(FOX + RET_W, C_FF, G_PRE), (2 * RET_W, C_RK, G_PRE), (RET_W, C_RZ, G_PRE), (2 * MEM_W, 0, G_MEM),
          (MEM_W, C_MQ, G_PRE), (MEM_W, C_MZ, G_PRE), (FOX_W, 0, G_PRE), (FOX_W, FOX_W, G_PRE),
          (FOX_W, 2 * FOX_W, G_PRE), (FOX_W, 3 * FOX_W, G_PRE), (512, 0, G_ONE), (512, 512, G_ONE)]
NCH = len(CHUNKS)

_USES = [("ffrq", NT), ("rkrv", NT), ("rz", NT), ("mk", 2), ("mv", NMT), ("mq", 4), ("mz", NT), ("mo", MEM),
         ("fq", 8), ("fk", 8), ("fv", NT), ("fo", FOX), ("fz", NT), ("wo0", NT), ("wo1", NT)]
PJ = {}
N_PJ = 0
for _n, _c in _USES:
    PJ[_n] = N_PJ
    N_PJ += _c
assert N_PJ % 2 == 0

TR_NORM = 0
TR_RET = TR_NORM + 2 * NT
TR_F = TR_RET + 2 * NT
TR_MEM = TR_F + 2
TR_ATT = TR_MEM + 2 * NMT

GRP = 4
ITEMS = [(0, h, t, GRP, NMT) for h in range(MEM) for t in range(0, NT, GRP)] + \
        [(1, h, t, 1, t + 1) for h in range(FOX) for t in range(NT)]
N_MI = MEM * NT // GRP
N_FI = FOX * NT
N_IT = len(ITEMS)
ITEM_TR = []
_u = TR_ATT
for _it in ITEMS:
    ITEM_TR.append(list(range(_u, _u + (_it[3] * _it[4] + 3) // 4)))
    _u += (_it[3] * _it[4] + 3) // 4
TR_Y = _u
N_TR = TR_Y + 2 * NT
assert N_TR % 2 == 0 and N_IT % 2 == 0

CR = 2


def n_full(u):
    return u - min(max(u - PJ["mo"], 0), MEM) - min(max(u - PJ["fo"], 0), FOX)


N_FULL = n_full(N_PJ)


def n_hi(u):
    return u - min(max(u - TR_RET, 0), TR_MEM - TR_RET)


N_HI = n_hi(N_TR)
SPLIT = [PJ["mk"], PJ["mk"] + 1] + [PJ["mv"] + i for i in range(NMT)] + [PJ["mq"] + i for i in range(4)] + \
        [PJ["fq"] + i for i in range(8)] + [PJ["fk"] + i for i in range(8)] + [PJ["fv"] + i for i in range(NT)]
N_SPLIT = len(SPLIT)
NAT = [(PJ["mk"] + i, 8) for i in range(2)] + [(PJ["mq"] + i, 4) for i in range(4)] + \
      [(PJ["fq"] + i, 4) for i in range(8)] + [(PJ["fk"] + i, 8) for i in range(8)]
NAT_AT = {u: v for v, (u, _) in enumerate(NAT)}
NAT_LAYER = 16 * sum(n for v, (_, n) in enumerate(NAT) if v % 2 == 0)
assert NAT_LAYER == 16 * sum(n for v, (_, n) in enumerate(NAT) if v % 2 == 1)


def nat_count(u):
    v = NAT_AT[u]
    return 16 * sum(n for w, (_, n) in enumerate(NAT) if w <= v and w % 2 == v % 2)


OUT_LAYER = 16 * (NT // 2)
N_Z = 3 * NT
N_SS = NMT + 2 * NT


def build(nc, x, mem, w_in, b_f, w_out, w_mkv, g_pre, g_post, g_mem, tables, out):
    ctx = ExitStack()
    with ctx:
        def sb(name, shape, dt=F32):
            return ctx.enter_context(nc.sbuf_tensor(name, shape, dt))

        def sem(name):
            return ctx.enter_context(nc.semaphore(name))

        hT = sb("hT", [P, 2, ND, S], F16)
        stage = sb("stage", [P, ND, 512])
        wp = sb("wp", [P, 2, 2, ND, 512], F16)
        y = sb("y", [P, NT, D])
        cb = sb("cb", [P, 2, S])
        tp = sb("tp", [P, 3, S])
        pt = sb("pt", [P, 2, 2, S], F16)
        region = sb("region", [P, 16384])
        tab = sb("tab", [P, 140])
        msk = sb("msk", [P, 2, P], BF16)
        fcol = sb("fcol", [P, NT, FOX])
        fabs = sb("fabs", [P, NT, FOX])
        gcol = sb("gcol", [P, 3, ND])
        gabs = sb("gabs", [P, 3, ND])
        bfb = sb("bfb", [P, FOX])
        rmax = sb("rmax", [P, ND])
        pmax = sb("pmax", [P, 1])
        amax = sb("amax", [P, 1])
        sval = sb("sval", [P, NCH])
        unsc = sb("unsc", [P, NCH])
        gs = sb("gs", [P, 2, ND])
        ssq = sb("ssq", [P, N_SS])
        msq = sb("msq", [P, N_SS])
        rstd = sb("rstd", [P, N_SS])
        negh = sb("negh", [P, 4])
        ones1 = sb("ones1", [P, 1])
        gss = sb("gss", [P, NT, 4])
        gms = sb("gms", [P, NT, 4])
        gnr = sb("gnr", [P, NT, 4])
        mxm = sb("mxm", [P, 4, GRP])
        nmm = sb("nmm", [P, 4, GRP])
        sc2 = sb("sc2", [P, 2, 3])
        mx = sb("mx", [P, 4])
        nm = sb("nm", [P, 4])
        rs = sb("rs", [P, 4, NT])
        rec = sb("rec", [P, 4, NT])
        ymax = sb("ymax", [P, NT])
        ysc = sb("ysc", [P, NT])
        yun = sb("yun", [P, NT])
        fo = sb("fo", [P, 2, NT])

        zeta_c, xi_c, dc_c = tab[:, 0:4], tab[:, 4:8], tab[:, 8:12]
        ident = tab[:, 12:140]
        ident_b, mask_b = msk[:, 0, :], msk[:, 1, :]

        def words(a, n, rows=P):
            return region[0:rows, a:a + n]

        xin = words(0, 8192).rearrange("p (t n) -> p t n", t=NT)
        memin = words(14336, 2048).rearrange("p (t n) -> p t n", t=NMT)
        rtab = words(0, 1024)
        cos_t, sin_t, decay_t = rtab[:, 0:256], rtab[:, 256:512], rtab[:, 512:1024]
        memT = words(12288, 2048).bitcast(F16).rearrange("p (a t n) -> p a t n", a=2, t=ND)
        qr = words(2048, 2048).rearrange("p (t n) -> p t n", t=NT)
        kr = words(4096, 512).rearrange("p (a n) -> p a n", a=2)
        kz = words(4608, 512).rearrange("p (a n) -> p a n", a=2)
        rv = words(5120, 512).rearrange("p (a n) -> p a n", a=2)
        rot = words(5632, 512).rearrange("p (a n) -> p a n", a=2)
        qkT = words(6144, 2048, HD).rearrange("p (a b n) -> p a b n", a=2, b=2)
        aT = words(8192, 1024).rearrange("p (a n) -> p a n", a=2)
        rcr = words(9216, 256)
        rsq = words(9472, 256)
        junk = words(9728, 1024)
        state = words(10752, 512, HD).rearrange("p (a n) -> p a n", a=2)
        ro = words(11264, 512).rearrange("p (a n) -> p a n", a=2)
        rst = words(11776, 256, HD)
        crow = words(8192, 1024, FOX)
        mqst = words(13056, 2048).bitcast(F16).rearrange("p (h n) -> p h n", h=MEM)
        mkst = words(15104, 1024).bitcast(F16).rearrange("p (h a n) -> p h a n", h=MEM, a=2)
        mvs = words(9728, 512).bitcast(F16).rearrange("p (a t n) -> p a t n", a=2, t=NMT)
        qst = words(0, 4096).bitcast(F16).rearrange("p (h n) -> p h n", h=FOX)
        kst = words(4096, 8192).bitcast(F16).rearrange("p (h a n) -> p h a n", h=FOX, a=2)
        fvs = words(12288, 4096).bitcast(F16).rearrange("p (a t n) -> p a t n", a=2, t=NT)
        ost = xin
        gpost = cb[:, 0, :]

        pj = ctx.enter_context(nc.psum_tensor("pj", [P, 2, 512], F32))
        tr = ctx.enter_context(nc.psum_tensor("tr", [P, 2, 512], F32))
        sp = ctx.enter_context(nc.psum_tensor("sp", [P, 2, S], F32))
        ret_a, ret_o, ret_kv = sp[:, 0, 0:512], sp[:, 0, 512:1024], sp[0:HD, 1, 0:256]

        def tr_bank(u):
            if TR_ATT <= u < TR_Y:
                k = (u - TR_ATT) % 3
                return pj[:, 1, :] if k == 2 else tr[:, k, :]
            return tr[:, u % 2, :]

        cdram = nc.dram_tensor("c_rows", (FOX, S), F32, kind="Internal").ap()

        held = sem("held")
        tab_in = sem("tab_in")
        w_in_sb = sem("w_in_sb")
        g_in = sem("g_in")
        gp_in = sem("gp_in")
        x_in = [sem(f"x_in{s}") for s in range(NT)]
        mem_in = sem("mem_in")
        rtab_in = sem("rtab_in")
        xr_in = [sem("xr_in0"), sem("xr_in1")]
        st_out = [sem("st_out0"), sem("st_out1")]
        stk_in = [sem("stk_in0"), sem("stk_in1")]
        res_in = [sem("res_in0"), sem("res_in1")]
        c_out = sem("c_out")
        cb_in = [sem("cb_in0"), sem("cb_in1")]
        consts = sem("consts")
        gabs_ok = sem("gabs_ok")
        amax_p = sem("amax_p")
        amax_a = sem("amax_a")
        w_scale = sem("w_scale")
        w_hi = sem("w_hi")
        w_ok = sem("w_ok")
        ss_ok = sem("ss_ok")
        rstd_ok = sem("rstd_ok")
        xh_ok = sem("xh_ok")
        pj_full = sem("pj_full")
        pj_hi = sem("pj_hi")
        pj_free = sem("pj_free")
        silu_ok = sem("silu_ok")
        tr_full = sem("tr_full")
        tr_hi = sem("tr_hi")
        tr_free = sem("tr_free")
        kr_ok = sem("kr_ok")
        ra_full = sem("ra_full")
        ra_ok = sem("ra_ok")
        rkv_full = sem("rkv_full")
        state_ok = sem("state_ok")
        ro_full = sem("ro_full")
        ro_free = sem("ro_free")
        gss_ok = sem("gss_ok")
        gnr_ok = sem("gnr_ok")
        fa_ok = sem("fa_ok")
        fl_ok = sem("fl_ok")
        fe_ok = sem("fe_ok")
        lf_ok = sem("lf_ok")
        crow_ok = sem("crow_ok")
        s_full = sem("s_full")
        s_free = sem("s_free")
        nm_ok = sem("nm_ok")
        p_ok = sem("p_ok")
        pv_done = sem("pv_done")
        ys_ok = sem("ys_ok")
        o_ok = sem("o_ok")
        out_ok = sem("out_ok")

        def chunk_src(l, c):
            width, c0, _ = CHUNKS[c]
            w = w_mkv if c == MKV else (w_out if c >= WO0 else w_in)
            return w.rearrange("l (p t) n -> l p t n", p=P)[l, :, :, c0:c0 + width]

        x_rows = x.rearrange("b (t p) d -> (b t) p d", p=P)
        mem_rows = mem.rearrange("b (t p) d -> (b t) p d", p=P)
        out_rows = out.rearrange("b (t p) d -> (b t) p d", p=P)

        def norm_rows(j):
            return xin[:, j, :] if j < NT else memin[:, j - NT, :]

        block = ctx.enter_context(nc.Block())

        @block.sync
        def _(q):
            def load_w(l, c):
                q.wait_ge(w_ok, l * NCH + c + 1)
                q.sem_inc(held, 1)
                q.dma_start(stage[:, :, 0:CHUNKS[c][0]], chunk_src(l, c)).then_inc(w_in_sb, 16)

            def spread(l, u, dst, k_like, head0, s0, n):
                slot = NAT_AT[u] % 2
                q.wait_ge(pj_free, l * N_PJ + u + 1 + CR)
                for b in range(2):
                    rows = slice(HD * b, HD * b + HD)
                    hi, lo = pt[rows, slot, 0, 0:n], pt[rows, slot, 1, 0:n]
                    h = head0 + b
                    if k_like:
                        for a, part in ((0, hi), (1, lo)):
                            for r in range(2):
                                q.dma_start(dst[HD * r:HD * r + HD, h, a, s0:s0 + n], part).then_inc(stk_in[slot], 16)
                    else:
                        q.dma_start(dst[0:HD, h, s0:s0 + n], hi).then_inc(stk_in[slot], 16)
                        q.dma_start(dst[HD:P, h, s0:s0 + n], lo).then_inc(stk_in[slot], 16)

            for s in range(NT):
                q.dma_start(xin[:, s, :], x_rows[s]).then_inc(x_in[s], 16)
                if s == 1:
                    q.dma_start(tab[:], tables[:, 0:140]).then_inc(tab_in, 16)
            q.dma_start(out_rows[0:NT // 2], x_rows[0:NT // 2]).then_inc(res_in[0], 16)
            q.dma_start(out_rows[NT // 2:NT], x_rows[NT // 2:NT]).then_inc(res_in[1], 16)
            with q.Fori(0, DEPTH) as l:
                load_w(l, FFRQ)
                for g, src in ((G_PRE, g_pre), (G_MEM, g_mem)):
                    q.dma_start(gcol[:, g, :], src.rearrange("l (p t) -> l p t", p=P)[l]).then_inc(g_in, 16)
                q.dma_start(bfb[:], b_f[l].partition_broadcast(P)).then_inc(g_in, 16)
                q.dma_start(memin, mem.rearrange("b (t p) d -> p (b t) d", p=P)).then_inc(mem_in, 16)
                q.wait_ge(tr_free, l * N_TR + 2 + CR)
                q.dma_start(rtab, tables[:, 140:1164]).then_inc(rtab_in, 16)
                load_w(l, RKRV)
                load_w(l, RZ)
                load_w(l, MKV)
                load_w(l, MQ)
                for i in range(2):
                    spread(l, PJ["mk"] + i, mkst, True, 2 * i, 0, N_MEM)
                load_w(l, MZ)
                for i in range(4):
                    spread(l, PJ["mq"] + i, mqst, False, 2 * (i // 2), 512 * (i % 2), 512)
                load_w(l, FQ)
                load_w(l, FK)
                for i in range(8):
                    spread(l, PJ["fq"] + i, qst, False, 2 * (i // 2), 512 * (i % 2), 512)
                load_w(l, FV)
                q.wait_ge(crow_ok, l + 1)
                q.dma_start(cdram, crow).then_inc(c_out, 16)
                q.wait_ge(c_out, l * 16 + 16)
                for h in range(2):
                    q.dma_start(cb[:, h, :], cdram[h].partition_broadcast(P)).then_inc(cb_in[h], 16)
                for i in range(8):
                    spread(l, PJ["fk"] + i, kst, True, 2 * (i // 2), 512 * (i % 2), 512)
                load_w(l, FZ)
                load_w(l, WO0)
                for h in range(2, FOX):
                    q.wait_ge(s_free, l * N_FI + NT * (h - 1) + CR)
                    q.dma_start(cb[:, h % 2, :], cdram[h].partition_broadcast(P)).then_inc(cb_in[h % 2], 16)
                q.wait_ge(s_free, l * N_FI + N_FI + CR)
                q.dma_start(gpost, g_post[l].partition_broadcast(P)).then_inc(gp_in, 16)
                load_w(l, WO1)
                q.wait_ge(pj_free, l * N_PJ + PJ["wo0"] + CR)
                q.sem_inc(held, 1)
                for i in range(2):
                    q.wait_ge(res_in[i], 16)
                    q.wait_ge(st_out[i], l * OUT_LAYER + OUT_LAYER)
                    q.sem_inc(held, 1)
                for s in range(2):
                    q.dma_start(tp[:, s, :], out_rows[s]).then_inc(xr_in[s], 16)
            for i in range(2):
                q.wait_ge(st_out[i], OUT_LAYER + DEPTH * OUT_LAYER)
            q.wait_ge(c_out, 16 * DEPTH)

        @block.gpsimd
        def _(pool):
            pool.memset(negh[:], -0.5)
            pool.memset(msk[:], 0.0)
            pool.drain()
            pool.affine_select(out=ident_b, in_=ident_b, compare_op=ALU.not_equal, fill=1.0, base=0,
                               pattern=[[-1, P]], channel_multiplier=1)
            pool.affine_select(out=mask_b, in_=mask_b, compare_op=ALU.is_ge, fill=-1e30, base=0,
                               pattern=[[-1, P]], channel_multiplier=1)
            pool.drain()
            pool.memset(ones1[:], 1.0)
            pool.memset(gcol[:, G_ONE, :], 1.0).then_inc(consts, 1)

            def chunk_max(l, c):
                pool.wait_ge(amax_p, l * NCH + c + 1)
                pool.sem_inc(held, 1)
                pool.partition_all_reduce(amax[:], pmax[:], P, RMAX).then_inc(amax_a, 1)

            def inv_rms(l, j):
                pool.wait_ge(ss_ok, l * N_SS + j + 1)
                pool.sem_inc(held, 1)
                pool.tensor_scalar(msq[:, j:j + 1], ssq[:, j:j + 1], 1.0 / D, EPS, ALU.mult, ALU.add)
                pool.drain()
                pool.tensor_tensor(rstd[:, j:j + 1], msq[:, j:j + 1], negh[:, 0:1], ALU.pow).then_inc(rstd_ok, 1)

            pool.wait_ge(consts, 1)
            with pool.Fori(0, DEPTH) as l:
                for j in range(NMT + NT):
                    inv_rms(l, j)
                    if j == 3:
                        chunk_max(l, FFRQ)
                chunk_max(l, RKRV)
                chunk_max(l, RZ)
                for s in range(NT):
                    pool.wait_ge(gss_ok, l * NT + s + 1)
                    pool.sem_inc(held, 1)
                    pool.tensor_scalar(gms[:, s, :], gss[:, s, :], 1.0 / HD, EPS, ALU.mult, ALU.add)
                    pool.drain()
                    pool.tensor_tensor(gnr[:, s, :], gms[:, s, :], negh[:], ALU.pow).then_inc(gnr_ok, 1)
                for c in range(MKV, NCH):
                    chunk_max(l, c)
                for j in range(NMT + NT, N_SS):
                    inv_rms(l, j)

        @block.scalar
        def _(act):
            def prep(l, c, k):
                if not 3 <= k <= 6:
                    return
                width, slot = CHUNKS[c][0], c % 2
                if k == 3:
                    act.wait_ge(w_scale, l * NCH + c + 1)
                    if c >= 2:
                        act.wait_ge(pj_full, l * N_FULL + n_full(LAST[c - 2] + 1))
                for dt in (2 * (k - 3), 2 * (k - 3) + 1):
                    last = act.activation(wp[:, slot, 0, dt, 0:width], stage[:, dt, 0:width], ACT.Copy,
                                          scale=gs[:, slot, dt:dt + 1])
                last.then_inc(w_hi, 1)

            def split_hi(l, u, dst, n):
                act.wait_ge(pj_full, l * N_FULL + n_full(u) + 1)
                if u in NAT_AT and NAT_AT[u] >= 2:
                    prev = NAT[NAT_AT[u] - 2][0]
                    act.wait_ge(stk_in[NAT_AT[u] % 2], l * NAT_LAYER + nat_count(prev))
                act.activation(dst, pj[:, u % 2, 0:n], ACT.Copy).then_inc(pj_hi, 1)

            def tr_split_hi(l, u, dst, shape_t):
                act.wait_ge(tr_full, l * N_TR + u + 1)
                n = shape_t * P
                src = tr_bank(u)[:, 0:n]
                if len(dst.shape) == 3:
                    src = src.rearrange("p (t n) -> p t n", t=shape_t)
                act.activation(dst, src, ACT.Copy).then_inc(tr_hi, 1)

            def silu(l, u, c, width, dst=None):
                act.wait_ge(pj_full, l * N_FULL + n_full(u) + 1)
                act.activation(tp[:, u % 2, 0:width] if dst is None else dst, pj[:, u % 2, 0:width], ACT.Silu,
                               scale=unsc[:, c:c + 1]).then_inc(silu_ok, 1)

            def attend(l, i0, n_items):
                for i in range(i0, i0 + n_items + 1):
                    if i < i0 + n_items:
                        kind, h, t, nt, nk = ITEMS[i]
                        act.wait_ge(nm_ok, l * N_IT + i + 1)
                        n = nk * P
                        for j in range(nt):
                            src = tp[:, i % 3, 0:n] if kind else sp[:, i % 2, j * n:j * n + n]
                            bias = nm[:, i % 4:i % 4 + 1] if kind else nmm[:, i % 4, j:j + 1]
                            last = act.activation(tp[:, i % 3, j * n:j * n + n], src, ACT.Exp, bias=bias,
                                                  scale=sc2[:, kind, 0:1], accum_out=rs[:, h % 4, t + j:t + j + 1])
                        last.then_inc(p_ok, 1)
                    if i > i0:
                        j = i - 1
                        nb = ITEMS[j][3] * ITEMS[j][4]
                        if j - 2 >= i0:
                            act.wait_ge(pv_done, l * N_IT + j - 1)
                        for b, u in enumerate(ITEM_TR[j]):
                            w = min(4, nb - 4 * b)
                            tr_split_hi(l, u, pt[:, j % 2, 0, 512 * b:512 * b + w * P], w)

            act.wait_ge(tab_in, 16)
            with act.Fori(0, DEPTH) as l:
                def squares(j):
                    if j < NT:
                        act.wait_ge(x_in[j], 16)
                        act.wait_ge(out_ok, l * NT + j + 1)
                    elif j == NT:
                        act.wait_ge(mem_in, l * 16 + 16)
                    if j >= 1:
                        act.wait_ge(ss_ok, l * N_SS + j)
                    act.activation(junk, norm_rows(j), ACT.Square, accum_out=ssq[:, j:j + 1]).then_inc(ss_ok, 1)

                def store(l, s):
                    act.wait_ge(out_ok, l * NT + s + 1 + NT)
                    act.dma_start(out_rows[s], xin[:, s, :]).then_inc(st_out[s % 2], 16)
                    if s + 2 < NT:
                        act.dma_start(tp[:, s % 2, :], out_rows[s + 2]).then_inc(xr_in[s % 2], 16)

                squares(0)
                squares(1)
                for j in range(NT):
                    squares(j + 2)
                    for b in range(2):
                        tr_split_hi(l, TR_NORM + 2 * j + b, hT[:, 0, 4 * b:4 * b + 4, j * P:j * P + P], 4)
                    if j >= 1:
                        prep(l, FFRQ, j - 1)
                for k in range(NT):
                    prep(l, RKRV, k)
                for k in range(NT):
                    prep(l, RZ, k)
                act.wait_ge(fa_ok, l + 1)
                act.activation(fabs[:], fabs[:], ACT.Exp, scale=-1.0).then_inc(fe_ok, 1)
                act.wait_ge(fe_ok, l + 1)
                act.activation(fabs[:], fabs[:], ACT.Ln, bias=1.0).then_inc(fl_ok, 1)
                for s in range(NT):
                    silu(l, PJ["rz"] + s, RZ, RET_W)
                    prep(l, MKV, s)
                    if 2 <= s < 2 + NMT:
                        for b in range(2):
                            tr_split_hi(l, TR_MEM + 2 * (s - 2) + b,
                                        memT[:, 0, 4 * b:4 * b + 4, (s - 2) * P:(s - 1) * P], 4)
                for i in range(2 + NMT):
                    u = PJ["mk"] + i
                    if i < 2:
                        split_hi(l, u, pt[:, NAT_AT[u] % 2, 0, 0:N_MEM], N_MEM)
                    else:
                        split_hi(l, u, mvs[:, 0, i - 2, :], MEM_W)
                    prep(l, MQ, 2 * i)
                    prep(l, MQ, 2 * i + 1)
                for i in range(4):
                    u = PJ["mq"] + i
                    split_hi(l, u, pt[:, NAT_AT[u] % 2, 0, 0:512], 512)
                    prep(l, MZ, 2 * i)
                    prep(l, MZ, 2 * i + 1)
                for s in range(NT):
                    silu(l, PJ["mz"] + s, MZ, MEM_W, y[:, s, FOX_W + RET_W:D])
                    prep(l, FQ, s)
                attend(l, 0, N_MI)
                for i in range(8):
                    u = PJ["fq"] + i
                    split_hi(l, u, pt[:, NAT_AT[u] % 2, 0, 0:512], 512)
                    prep(l, FK, i)
                for i in range(8):
                    u = PJ["fk"] + i
                    split_hi(l, u, pt[:, NAT_AT[u] % 2, 0, 0:512], 512)
                    prep(l, FV, i)
                for s in range(NT):
                    split_hi(l, PJ["fv"] + s, fvs[:, 0, s, :], FOX_W)
                    prep(l, FZ, s)
                attend(l, N_MI, N_IT - N_MI)
                for s in range(NT + 1):
                    if s < NT:
                        silu(l, PJ["fz"] + s, FZ, FOX_W)
                        prep(l, WO0, s)
                    if s >= 1:
                        for b in range(2):
                            tr_split_hi(l, TR_Y + 2 * (s - 1) + b, hT[:, 0, 4 * b:4 * b + 4, (s - 1) * P:s * P], 4)
                for s in range(NT):
                    prep(l, WO1, s)
                for s in range(NT):
                    j = NMT + NT + s
                    act.wait_ge(o_ok, l * NT + s + 1)
                    act.wait_ge(ss_ok, l * N_SS + j)
                    act.activation(words(8192, 1024), ost[:, s, :], ACT.Square,
                                   accum_out=ssq[:, j:j + 1]).then_inc(ss_ok, 1)
                    if s >= 1:
                        store(l, s - 1)
                store(l, NT - 1)

        @block.tensor
        def _(pe):
            def open_unit(l, u):
                after_o = u - 1 in range(PJ["mo"], PJ["mo"] + MEM) or u - 1 in range(PJ["fo"], PJ["fo"] + FOX)
                pe.wait_ge(pj_free, l * N_PJ + u + (2 if after_o else 1))

            def rows_unit(l, u, c, lhs, t, c0, n, tiles=(0, ND)):
                if tiles[0] == 0:
                    open_unit(l, u)
                for dt in range(*tiles):
                    for a, b in ((0, 0), (0, 1), (1, 0)):
                        last = pe.matmul(pj[:, u % 2, 0:n], lhs[:, a, dt, t * P:t * P + P],
                                         wp[:, c % 2, b, dt, c0:c0 + n],
                                         start=(dt == 0 and a + b == 0), stop=(dt == ND - 1 and a == 1))
                if tiles[1] == ND:
                    last.then_inc(pj_full, 1)

            def cols_unit(l, u, c, rhs, e0, s0, n):
                open_unit(l, u)
                for dt in range(ND):
                    for a, b in ((0, 0), (0, 1), (1, 0)):
                        last = pe.matmul(pj[:, u % 2, 0:n], wp[:, c % 2, a, dt, e0:e0 + P],
                                         rhs[:, b, dt, s0:s0 + n],
                                         start=(dt == 0 and a + b == 0), stop=(dt == ND - 1 and a == 1))
                last.then_inc(pj_full, 1)

            def chunk_ready(l, c):
                pe.wait_ge(w_ok, l * NCH + c + 2)

            def transposes(l, u, srcs, rows=P):
                pe.wait_ge(tr_free, l * N_TR + u + (0 if TR_ATT <= u < TR_Y else 1))
                if rows != P:
                    pe.sem_inc(held, 1)
                for k, src in enumerate(srcs):
                    last = pe.transpose(tr_bank(u)[0:rows, k * P:k * P + P], src, ident)
                last.then_inc(tr_full, 1)

            def ret_out(l, s):
                pe.wait_ge(ra_ok, l * NT + s + 1)
                if s > 0:
                    pe.wait_ge(state_ok, l * NT + s)
                    pe.wait_ge(ro_free, l * NT + s)
                r = s % 2
                for h in range(RET):
                    e = slice(h * HD, h * HD + HD)
                    last = pe.matmul(ret_o[:, e], aT[:, r, h * P:h * P + P], rv[:, r, e], start=True, stop=True)
                if s > 0:
                    for h in range(RET):
                        e = slice(h * HD, h * HD + HD)
                        last = pe.matmul(ret_o[:, 256 + h * HD:256 + h * HD + HD], qkT[:, r, 0, h * P:h * P + P],
                                         state[:, r, e], start=True, stop=True)
                last.then_inc(ro_full, 1)

            def ret_transposes(l, s):
                pe.wait_ge(kr_ok, l * NT + s + 1)
                transposes(l, TR_RET + 2 * s, [qr[:, s, h * HD:h * HD + HD] for h in range(RET)], HD)
                transposes(l, TR_RET + 2 * s + 1, [kr[:, s % 2, h * HD:h * HD + HD] for h in range(RET)], HD)

            def ret_scores(l, s):
                r = s % 2
                pe.wait_ge(tr_free, l * N_TR + TR_RET + 2 * s + 2 + CR)
                for h in range(RET):
                    last = pe.matmul(ret_a[:, h * P:h * P + P], qkT[:, r, 1, h * P:h * P + P],
                                     qkT[:, r, 0, h * P:h * P + P], start=True, stop=True)
                last.then_inc(ra_full, 1)
                if s > 0:
                    pe.wait_ge(state_ok, l * NT + s)
                for h in range(RET):
                    e = slice(h * HD, h * HD + HD)
                    last = pe.matmul(ret_kv[:, e], kz[:, r, e], rv[:, r, e], start=True, stop=True)
                last.then_inc(rkv_full, 1)

            def item_scores(l, i):
                kind, h, t, nt, nk = ITEMS[i]
                if kind:
                    pe.wait_ge(s_free, l * N_FI + i - N_MI + 1)
                elif i >= 2:
                    pe.wait_ge(p_ok, l * N_IT + i - 1)
                k = kst if kind else mkst
                for j in range(nt):
                    q = (qst if kind else mqst)[:, h, (t + j) * P:(t + j + 1) * P]
                    for a in range(0, nk * P, 512):
                        n = min(512, nk * P - a)
                        c0 = j * nk * P + a
                        o = sp[:, i % 2, c0:c0 + n]
                        diag = kind and a + n == nk * P
                        pe.matmul(o, q, k[:, h, 0, a:a + n], start=True, stop=False)
                        last = pe.matmul(o, q, k[:, h, 1, a:a + n], start=False, stop=not diag)
                        if diag:
                            last = pe.matmul(sp[:, i % 2, a + n - P:a + n], ident_b, mask_b, start=False, stop=True)
                last.then_inc(s_full, 1)

            def item_transposes(l, i):
                pe.wait_ge(p_ok, l * N_IT + i + 1)
                nb = ITEMS[i][3] * ITEMS[i][4]
                for b, u in enumerate(ITEM_TR[i]):
                    transposes(l, u, [tp[:, i % 3, k * P:k * P + P] for k in range(4 * b, min(nb, 4 * b + 4))])

            def item_values(l, i):
                kind, h, t, nt, nk = ITEMS[i]
                u = (PJ["fo"] if kind else PJ["mo"]) + h
                if t == 0:
                    open_unit(l, u)
                pe.wait_ge(tr_free, l * N_TR + ITEM_TR[i][-1] + 1 + CR)
                v = fvs if kind else mvs
                e = slice(h * HD, h * HD + HD)
                for j in range(nt):
                    o = pj[:, 0, (t + j) * HD:(t + j + 1) * HD]
                    for k in range(nk):
                        p0 = (j * nk + k) * P
                        for a, b in ((0, 0), (0, 1), (1, 0)):
                            last = pe.matmul(o, pt[:, i % 2, a, p0:p0 + P], v[:, b, k, e],
                                             start=(k == 0 and a + b == 0), stop=(k == nk - 1 and a == 1))
                last.then_inc(pv_done, 1)

            def attend(l, i0, n_items):
                end = i0 + n_items
                pe.wait_ge(pj_free, l * N_PJ + PJ["fo" if ITEMS[i0][0] else "mo"] + CR)
                pe.wait_ge(tr_free, l * N_TR + ITEM_TR[i0][0] + CR)
                item_scores(l, i0)
                item_scores(l, i0 + 1)
                for i in range(i0, end + 2):
                    if i + 2 < end:
                        item_scores(l, i + 2)
                    if i0 <= i - 2:
                        item_values(l, i - 2)
                    if i < end:
                        item_transposes(l, i)

            pe.wait_ge(consts, 1)
            pe.wait_ge(tab_in, 16)
            with pe.Fori(0, DEPTH) as l:
                def norm_transposes(j, u):
                    pe.wait_ge(xh_ok, l * (NMT + NT) + j + 1)
                    for b in range(2):
                        transposes(l, u + b, [norm_rows(j)[:, k:D:ND] for k in range(4 * b, 4 * b + 4)])

                for j in range(NT):
                    norm_transposes(j, TR_NORM + 2 * j)
                pe.wait_ge(tr_free, l * N_TR + TR_RET + CR)
                chunk_ready(l, FFRQ)
                for s in range(NT):
                    rows_unit(l, PJ["ffrq"] + s, FFRQ, hT, s, 0, FOX + RET_W)
                chunk_ready(l, RKRV)
                for s in range(NT + 2):
                    if s < NT:
                        rows_unit(l, PJ["rkrv"] + s, RKRV, hT, s, 0, 2 * RET_W, (0, ND // 2))
                    if 1 <= s <= NT:
                        ret_transposes(l, s - 1)
                    if s >= 2:
                        ret_out(l, s - 2)
                    if s < NT:
                        rows_unit(l, PJ["rkrv"] + s, RKRV, hT, s, 0, 2 * RET_W, (ND // 2, ND))
                    if 1 <= s <= NT:
                        ret_scores(l, s - 1)
                pe.wait_ge(lf_ok, l + 1)
                for b in range(2):
                    transposes(l, TR_F + b, [fcol[:, s, :] for s in range(4 * b, 4 * b + 4)], FOX)
                chunk_ready(l, RZ)
                for s in range(NT):
                    rows_unit(l, PJ["rz"] + s, RZ, hT, s, 0, RET_W)
                    if 2 <= s < 2 + NMT:
                        norm_transposes(NT + s - 2, TR_MEM + 2 * (s - 2))
                pe.wait_ge(tr_free, l * N_TR + TR_ATT + CR)
                chunk_ready(l, MKV)
                for i in range(2):
                    cols_unit(l, PJ["mk"] + i, MKV, memT, i * P, 0, N_MEM)
                for i in range(NMT):
                    rows_unit(l, PJ["mv"] + i, MKV, memT, i, MEM_W, MEM_W)
                chunk_ready(l, MQ)
                for i in range(4):
                    cols_unit(l, PJ["mq"] + i, MQ, hT, (i // 2) * P, 512 * (i % 2), 512)
                chunk_ready(l, MZ)
                for s in range(NT):
                    rows_unit(l, PJ["mz"] + s, MZ, hT, s, 0, MEM_W)
                for b in range(2):
                    pe.wait_ge(stk_in[b], l * NAT_LAYER + nat_count(PJ["mq"] + 2 + (b - NAT_AT[PJ["mq"] + 2]) % 2))
                attend(l, 0, N_MI)
                chunk_ready(l, FQ)
                for i in range(8):
                    cols_unit(l, PJ["fq"] + i, FQ, hT, (i // 2) * P, 512 * (i % 2), 512)
                chunk_ready(l, FK)
                for i in range(8):
                    cols_unit(l, PJ["fk"] + i, FK, hT, (i // 2) * P, 512 * (i % 2), 512)
                chunk_ready(l, FV)
                for s in range(NT):
                    rows_unit(l, PJ["fv"] + s, FV, hT, s, 0, FOX_W)
                for b in range(2):
                    pe.wait_ge(stk_in[b], l * NAT_LAYER + NAT_LAYER)
                attend(l, N_MI, N_IT - N_MI)
                chunk_ready(l, FZ)
                for s in range(NT + 1):
                    if s < NT:
                        rows_unit(l, PJ["fz"] + s, FZ, hT, s, 0, FOX_W)
                    if s >= 1:
                        pe.wait_ge(ys_ok, l * NT + s)
                        for b in range(2):
                            transposes(l, TR_Y + 2 * (s - 1) + b,
                                       [y[:, s - 1, k:D:ND] for k in range(4 * b, 4 * b + 4)])
                chunk_ready(l, WO0)
                pe.wait_ge(tr_free, l * N_TR + N_TR + CR)
                for s in range(NT):
                    rows_unit(l, PJ["wo0"] + s, WO0, hT, s, 0, 512)
                chunk_ready(l, WO1)
                for s in range(NT):
                    rows_unit(l, PJ["wo1"] + s, WO1, hT, s, 0, 512)

        @block.vector
        def _(dve):
            def prep(l, c, k):
                width, _, g = CHUNKS[c]
                slot = c % 2
                if k < 2:
                    if k == 0:
                        dve.wait_ge(w_in_sb, l * 16 * NCH + 16 * c + 16)
                    dve.tensor_reduce(rmax[:, 4 * k:4 * k + 4], stage[:, 4 * k:4 * k + 4, 0:width], AX.X, ALU.max,
                                      apply_absolute_value=True)
                if k == 1:
                    dve.drain()
                    dve.tensor_tensor(rmax[:], rmax[:], gabs[:, g, :], ALU.mult)
                    dve.drain()
                    dve.tensor_reduce(pmax[:], rmax[:], AX.X, ALU.max).then_inc(amax_p, 1)
                if k == 2:
                    dve.wait_ge(amax_a, l * NCH + c + 1)
                    dve.tensor_scalar(amax[:], amax[:], 2.0 ** -30, None, ALU.max)
                    dve.drain()
                    power_of_two(sval[:, c:c + 1], unsc[:, c:c + 1], amax[:])
                    dve.tensor_scalar(gs[:, slot, :], gcol[:, g, :], sval[:, c:c + 1], None,
                                      ALU.mult).then_inc(w_scale, 1)
                if 3 <= k <= 6:
                    if k == 3:
                        dve.drain()
                    dve.wait_ge(w_hi, l * 4 * NCH + 4 * c + k - 2)
                    for dt in (2 * (k - 3), 2 * (k - 3) + 1):
                        last = dve.scalar_tensor_tensor(wp[:, slot, 1, dt, 0:width], stage[:, dt, 0:width],
                                                        gs[:, slot, dt:dt + 1], wp[:, slot, 0, dt, 0:width],
                                                        ALU.mult, ALU.subtract)
                    if k == 6:
                        last.then_inc(w_ok, 1)

            def power_of_two(up, down, m):
                dve.tensor_scalar(down.bitcast(I32), m.bitcast(I32), 0x7F800000, None, ALU.bitwise_and)
                dve.drain()
                dve.tensor_scalar(up.bitcast(I32), down.bitcast(I32), -1.0, float(0x7F000000), ALU.mult, ALU.add)
                dve.drain()

            def split_lo(l, u, hi, lo, n):
                dve.wait_ge(pj_hi, l * N_SPLIT + SPLIT.index(u) + 1)
                dve.tensor_tensor(lo, pj[:, u % 2, 0:n], hi, ALU.subtract).then_inc(pj_free, 1)

            def tr_split_lo(l, u, hi, lo, w):
                dve.wait_ge(tr_hi, l * N_HI + n_hi(u) + 1)
                src = tr_bank(u)[:, 0:w * P]
                if len(hi.shape) == 3:
                    src = src.rearrange("p (t n) -> p t n", t=w)
                dve.tensor_tensor(lo, src, hi, ALU.subtract).then_inc(tr_free, 1)

            def gate(l, u, z, s, c0, width):
                dve.wait_ge(silu_ok, l * N_Z + z + 1)
                yv = y[:, s, c0:c0 + width]
                dve.tensor_tensor(yv, yv, tp[:, u % 2, 0:width], ALU.mult).then_inc(pj_free, 1)

            def rotary(src, dst, scale):
                s8 = src.rearrange("p (h j) -> p h j", j=32)
                dve.scalar_tensor_tensor(rot[:, 0, :].rearrange("p (h j) -> p h j", j=32), s8, scale, cos_now,
                                         ALU.mult, ALU.mult)
                last = dve.scalar_tensor_tensor(rot[:, 1, :].rearrange("p (h j) -> p h j", j=32), s8, scale, sin_now,
                                                ALU.mult, ALU.mult)
                return last

            def rotary_sum(dst):
                t1 = rot[:, 0, :].rearrange("p (h two j) -> p h two j", two=2, j=32)
                t2 = rot[:, 1, :].rearrange("p (h two j) -> p h two j", two=2, j=32)
                d = dst.rearrange("p (h two j) -> p h two j", two=2, j=32)
                dve.tensor_tensor(d[:, :, 0, :], t1[:, :, 0, :], t2[:, :, 1, :], ALU.subtract)
                return dve.tensor_tensor(d[:, :, 1, :], t1[:, :, 1, :], t2[:, :, 0, :], ALU.add)

            def heads(ap):
                return ap.rearrange("p (h e) -> p h e", h=RET)

            def over_head(col, n=P):
                return col.unsqueeze(2).to_broadcast([n, RET, HD])

            def item_max(l, i, i0):
                kind, h, t, nt, nk = ITEMS[i]
                n = nk * P
                dve.wait_ge(s_full, l * N_IT + i + 1)
                if not kind:
                    dve.tensor_reduce(mxm[:, i % 4, :], sp[:, i % 2, :].rearrange("p (t n) -> p t n", t=nt), AX.X,
                                      ALU.max)
                    dve.drain()
                    dve.tensor_scalar(nmm[:, i % 4, :], mxm[:, i % 4, :], sc2[:, kind, 1:2], None,
                                      ALU.mult).then_inc(nm_ok, 1)
                    return
                if i - 3 >= i0:
                    dve.wait_ge(tr_full, l * N_TR + ITEM_TR[i - 3][-1] + 1)
                if t == 0:
                    dve.wait_ge(cb_in[h % 2], l * 16 * (FOX // 2) + 16 * (h // 2) + 16)
                dve.sem_inc(held, 1)
                dve.tensor_tensor_reduce(tp[:, i % 3, 0:n], sp[:, i % 2, 0:n], cb[:, h % 2, 0:n], 1.0, -3.0e38, ALU.add, ALU.max,
                                         mx[:, i % 4:i % 4 + 1]).then_inc(s_free, 1)
                dve.drain()
                dve.tensor_scalar(nm[:, i % 4:i % 4 + 1], mx[:, i % 4:i % 4 + 1], sc2[:, kind, 1:2], None,
                                  ALU.mult).then_inc(nm_ok, 1)

            def head_out(l, i):
                kind, h = ITEMS[i][0:2]
                u = (PJ["fo"] if kind else PJ["mo"]) + h
                c = FV if kind else MKV
                c0 = (0 if kind else FOX_W + RET_W) + h * HD
                r = h % 4
                dve.wait_ge(pv_done, l * N_IT + i + 1)
                dve.reciprocal(rec[:, r, :], rs[:, r, :])
                dve.drain()
                dve.tensor_scalar(rec[:, r, :], rec[:, r, :], unsc[:, c:c + 1], None, ALU.mult)
                dve.drain()
                yv = y[:, :, c0:c0 + HD]
                o = pj[:, 0, :].rearrange("p (t e) -> p t e", t=NT)
                over_row = rec[:, r, :].unsqueeze(2).to_broadcast([P, NT, HD])
                if not kind:
                    dve.tensor_tensor(yv, yv, over_row, ALU.mult)
                    dve.drain()
                dve.tensor_tensor(yv, o, over_row if kind else yv, ALU.mult).then_inc(pj_free, 1)

            def attend(l, i0, n_items):
                end = i0 + n_items
                item_max(l, i0, i0)
                item_max(l, i0 + 1, i0)
                for i in range(i0, end + 2):
                    j = i - 1
                    if i0 <= j < end:
                        nb = ITEMS[j][3] * ITEMS[j][4]
                        for b, u in enumerate(ITEM_TR[j]):
                            w = min(4, nb - 4 * b)
                            sl = slice(512 * b, 512 * b + w * P)
                            tr_split_lo(l, u, pt[:, j % 2, 0, sl], pt[:, j % 2, 1, sl], w)
                    if i + 2 < end:
                        item_max(l, i + 2, i0)
                    if i0 <= i - 2 and ITEMS[i - 2][2] + ITEMS[i - 2][3] == NT:
                        head_out(l, i - 2)
                dve.drain()

            def attention_scale(kind, cq, ck):
                dve.tensor_scalar(sc2[:, kind, 0:1], unsc[:, cq:cq + 1], unsc[:, ck:ck + 1], HD ** -0.5,
                                  ALU.mult, ALU.mult)
                dve.tensor_scalar(sc2[:, kind, 2:3], sval[:, cq:cq + 1], sval[:, ck:ck + 1], -(HD ** 0.5),
                                  ALU.mult, ALU.mult)
                dve.drain()
                dve.tensor_scalar(sc2[:, kind, 1:2], sc2[:, kind, 0:1], -1.0, None, ALU.mult)
                dve.drain()

            dve.wait_ge(consts, 1)
            dve.sem_inc(pj_free, CR)
            dve.sem_inc(tr_free, CR)
            dve.sem_inc(s_free, CR)
            dve.sem_inc(w_ok, 1)
            dve.sem_inc(out_ok, NT)
            for i in range(2):
                dve.sem_inc(st_out[i], OUT_LAYER)
            dve.wait_ge(tab_in, 16)
            with dve.Fori(0, DEPTH) as l:
                dve.wait_ge(g_in, l * 48 + 48)
                dve.scalar_tensor_tensor(gabs[:], gcol[:], -1.0, gcol[:], ALU.mult, ALU.max).then_inc(gabs_ok, 1)
                def norm(j):
                    dve.wait_ge(rstd_ok, l * N_SS + j + 1)
                    if j < NT:
                        dve.wait_ge(st_out[j % 2], l * OUT_LAYER + 16 * (j // 2) + 16)
                    dve.tensor_scalar(norm_rows(j), norm_rows(j), rstd[:, j:j + 1], None, ALU.mult).then_inc(xh_ok, 1)

                norm(0)
                for j in range(NT):
                    if j + 1 < NT:
                        norm(j + 1)
                    for b in range(2):
                        cs = slice(j * P, j * P + P)
                        tr_split_lo(l, TR_NORM + 2 * j + b, hT[:, 0, 4 * b:4 * b + 4, cs],
                                    hT[:, 1, 4 * b:4 * b + 4, cs], 4)
                    if j >= 1:
                        prep(l, FFRQ, j - 1)
                dve.wait_ge(rtab_in, l * 16 + 16)
                dve.sem_inc(held, 1)
                for s in range(NT):
                    u = PJ["ffrq"] + s
                    dve.drain()
                    dve.wait_ge(pj_full, l * N_FULL + n_full(u) + 1)
                    cos_now = cos_t[:, 32 * s:32 * s + 32].unsqueeze(1).to_broadcast([P, 2 * RET, 32])
                    sin_now = sin_t[:, 32 * s:32 * s + 32].unsqueeze(1).to_broadcast([P, 2 * RET, 32])
                    dve.scalar_tensor_tensor(fcol[:, s, :], pj[:, u % 2, 0:FOX], unsc[:, FFRQ:FFRQ + 1], bfb[:],
                                             ALU.mult, ALU.add)
                    rotary(pj[:, u % 2, FOX:FOX + RET_W], None, unsc[:, FFRQ:FFRQ + 1]).then_inc(pj_free, 1)
                    dve.drain()
                    rotary_sum(qr[:, s, :])
                    prep(l, RKRV, s)
                dve.drain()
                dve.scalar_tensor_tensor(fabs[:], fcol[:], -1.0, fcol[:], ALU.mult, ALU.max).then_inc(fa_ok, 1)
                dve.tensor_scalar(sc2[:, 0, 0:1], unsc[:, RKRV:RKRV + 1], HD ** -0.5, None, ALU.mult)
                dve.drain()
                for s in range(NT + 3):
                    if 1 <= s <= NT:
                        n = s - 1
                        r = n % 2
                        for b in range(2):
                            u = TR_RET + 2 * n + b
                            dve.wait_ge(tr_full, l * N_TR + u + 1)
                            dve.tensor_copy(qkT[:, r, b, :], tr[0:HD, u % 2, :]).then_inc(tr_free, 1)
                    if 2 <= s < NT + 2:
                        n = s - 2
                        r = n % 2
                        dve.wait_ge(ro_full, l * NT + n + 1)
                        if n == 0:
                            dve.tensor_copy(ro[:, r, :], ret_o[:, 0:256]).then_inc(ro_free, 1)
                        else:
                            dve.tensor_tensor(heads(rcr), heads(ret_o[:, 256:512]), over_head(xi_c), ALU.mult)
                            dve.drain()
                            dve.tensor_tensor(ro[:, r, :], ret_o[:, 0:256], rcr, ALU.add).then_inc(ro_free, 1)
                        dve.drain()
                        dve.tensor_tensor(rsq, ro[:, r, :], ro[:, r, :], ALU.mult)
                        dve.drain()
                        dve.tensor_reduce(gss[:, n, :], heads(rsq), AX.X, ALU.add).then_inc(gss_ok, 1)
                    if s < NT:
                        u = PJ["rkrv"] + s
                        r = s % 2
                        dve.drain()
                        dve.wait_ge(pj_full, l * N_FULL + n_full(u) + 1)
                        cos_now = cos_t[:, 32 * s:32 * s + 32].unsqueeze(1).to_broadcast([P, 2 * RET, 32])
                        sin_now = sin_t[:, 32 * s:32 * s + 32].unsqueeze(1).to_broadcast([P, 2 * RET, 32])
                        rotary(pj[:, u % 2, 0:RET_W], None, sc2[:, 0, 0:1])
                        dve.tensor_scalar(rv[:, r, :], pj[:, u % 2, RET_W:2 * RET_W], unsc[:, RKRV:RKRV + 1], None,
                                          ALU.mult).then_inc(pj_free, 1)
                        dve.drain()
                        rotary_sum(kr[:, r, :])
                        dve.drain()
                        dve.tensor_tensor(heads(kz[:, r, :]), heads(kr[:, r, :]), over_head(zeta_c),
                                          ALU.mult).then_inc(kr_ok, 1)
                    if s >= 3:
                        n = s - 3
                        dve.wait_ge(gnr_ok, l * NT + n + 1)
                        dve.tensor_tensor(heads(y[:, n, FOX_W:FOX_W + RET_W]), heads(ro[:, n % 2, :]),
                                          over_head(gnr[:, n, :]), ALU.mult)
                    if 1 <= s <= NT:
                        n = s - 1
                        r = n % 2
                        dve.wait_ge(ra_full, l * NT + n + 1)
                        dve.tensor_tensor(aT[:, r, :], ret_a, decay_t, ALU.mult).then_inc(ra_ok, 1)
                        dve.wait_ge(rkv_full, l * NT + n + 1)
                        if n == 0:
                            dve.tensor_copy(state[:, 1, :], ret_kv).then_inc(state_ok, 1)
                        else:
                            dve.tensor_tensor(heads(rst), heads(state[:, r, :]), over_head(dc_c[0:HD, :], HD),
                                              ALU.mult)
                            dve.drain()
                            dve.tensor_tensor(state[:, 1 - r, :], rst, ret_kv, ALU.add).then_inc(state_ok, 1)
                    if s < NT:
                        prep(l, RZ, s)
                dve.wait_ge(fl_ok, l + 1)
                dve.scalar_tensor_tensor(fcol[:], fcol[:], 0.0, fabs[:], ALU.min, ALU.subtract).then_inc(lf_ok, 1)
                for b in range(2):
                    u = TR_F + b
                    dve.wait_ge(tr_full, l * N_TR + u + 1)
                    dve.tensor_tensor_scan(crow[:, 512 * b:512 * b + 512],
                                           ones1[0:FOX, :].to_broadcast([FOX, 512]), tr[0:FOX, u % 2, :],
                                           crow[:, 511:512] if b else 0.0, ALU.mult, ALU.add).then_inc(tr_free, 1)
                    dve.drain()
                norm(NT)
                norm(NT + 1)
                for s in range(NT):
                    gate(l, PJ["rz"] + s, s, s, FOX_W, RET_W)
                    prep(l, MKV, s)
                    if 2 <= s < 2 + NMT:
                        cs = slice((s - 2) * P, (s - 1) * P)
                        for b in range(2):
                            tr_split_lo(l, TR_MEM + 2 * (s - 2) + b, memT[:, 0, 4 * b:4 * b + 4, cs],
                                        memT[:, 1, 4 * b:4 * b + 4, cs], 4)
                for i in range(2 + NMT):
                    u = PJ["mk"] + i
                    if i < 2:
                        sl = NAT_AT[u] % 2
                        split_lo(l, u, pt[:, sl, 0, 0:N_MEM], pt[:, sl, 1, 0:N_MEM], N_MEM)
                    else:
                        split_lo(l, u, mvs[:, 0, i - 2, :], mvs[:, 1, i - 2, :], MEM_W)
                    prep(l, MQ, 2 * i)
                    prep(l, MQ, 2 * i + 1)
                for i in range(4):
                    sl = NAT_AT[PJ["mq"] + i] % 2
                    split_lo(l, PJ["mq"] + i, pt[:, sl, 0, 0:512], pt[:, sl, 1, 0:512], 512)
                    prep(l, MZ, 2 * i)
                    prep(l, MZ, 2 * i + 1)
                attention_scale(0, MQ, MKV)
                for s in range(NT):
                    dve.wait_ge(silu_ok, l * N_Z + NT + s + 1)
                    dve.sem_inc(pj_free, 1)
                    prep(l, FQ, s)
                attend(l, 0, N_MI)
                for i in range(8):
                    sl = NAT_AT[PJ["fq"] + i] % 2
                    split_lo(l, PJ["fq"] + i, pt[:, sl, 0, 0:512], pt[:, sl, 1, 0:512], 512)
                    prep(l, FK, i)
                attention_scale(1, FQ, FK)
                dve.tensor_scalar(crow, crow, sc2[0:FOX, 1, 2:3], None, ALU.mult).then_inc(crow_ok, 1)
                for i in range(8):
                    sl = NAT_AT[PJ["fk"] + i] % 2
                    split_lo(l, PJ["fk"] + i, pt[:, sl, 0, 0:512], pt[:, sl, 1, 0:512], 512)
                    prep(l, FV, i)
                for s in range(NT):
                    split_lo(l, PJ["fv"] + s, fvs[:, 0, s, :], fvs[:, 1, s, :], 512)
                    prep(l, FZ, s)
                attend(l, N_MI, N_IT - N_MI)
                for s in range(NT + 1):
                    if s < NT:
                        gate(l, PJ["fz"] + s, 2 * NT + s, s, 0, FOX_W)
                        dve.drain()
                        one = slice(s, s + 1)
                        dve.tensor_reduce(ymax[:, one], y[:, s, :], AX.X, ALU.max, apply_absolute_value=True)
                        dve.drain()
                        dve.tensor_scalar(ymax[:, one], ymax[:, one], 2.0 ** -30, None, ALU.max)
                        dve.drain()
                        power_of_two(ysc[:, one], yun[:, one], ymax[:, one])
                        dve.tensor_scalar(y[:, s, :], y[:, s, :], ysc[:, one], None, ALU.mult).then_inc(ys_ok, 1)
                        prep(l, WO0, s)
                    if s >= 1:
                        for b in range(2):
                            cs = slice((s - 1) * P, s * P)
                            tr_split_lo(l, TR_Y + 2 * (s - 1) + b, hT[:, 0, 4 * b:4 * b + 4, cs],
                                        hT[:, 1, 4 * b:4 * b + 4, cs], 4)
                dve.tensor_scalar(fo[:, 0, :], yun[:], unsc[:, WO0:WO0 + 1], None, ALU.mult)
                dve.drain()
                for s in range(NT):
                    u = PJ["wo0"] + s
                    dve.wait_ge(pj_full, l * N_FULL + n_full(u) + 1)
                    dve.tensor_scalar(ost[:, s, 0:512], pj[:, u % 2, :], fo[:, 0, s:s + 1], None,
                                      ALU.mult).then_inc(pj_free, 1)
                    prep(l, WO1, s)
                dve.tensor_scalar(fo[:, 1, :], yun[:], unsc[:, WO1:WO1 + 1], None, ALU.mult)
                dve.drain()
                dve.wait_ge(gp_in, l * 16 + 16)
                for s in range(NT + 1):
                    if s < NT:
                        u = PJ["wo1"] + s
                        dve.wait_ge(pj_full, l * N_FULL + n_full(u) + 1)
                        dve.tensor_scalar(ost[:, s, 512:1024], pj[:, u % 2, :], fo[:, 1, s:s + 1], None,
                                          ALU.mult).then_inc(pj_free, 1)
                        dve.drain().then_inc(o_ok, 1)
                    if s >= 1:
                        n = s - 1
                        j = NMT + NT + n
                        dve.wait_ge(rstd_ok, l * N_SS + j + 1)
                        dve.scalar_tensor_tensor(ost[:, n, :], ost[:, n, :], rstd[:, j:j + 1], gpost, ALU.mult,
                                                 ALU.mult)
                        dve.drain()
                        dve.wait_ge(xr_in[n % 2], l * 16 * (NT // 2) + 16 * (n // 2) + 16)
                        dve.tensor_tensor(ost[:, n, :], tp[:, n % 2, :], ost[:, n, :], ALU.add).then_inc(out_ok, 1)


LAST = {MKV: PJ["mv"] + NMT - 1, FFRQ: PJ["ffrq"] + 7, RKRV: PJ["rkrv"] + 7, RZ: PJ["rz"] + 7, MQ: PJ["mq"] + 3,
        MZ: PJ["mz"] + 7, FQ: PJ["fq"] + 7, FK: PJ["fk"] + 7, FV: PJ["fv"] + 7, FZ: PJ["fz"] + 7,
        WO0: PJ["wo0"] + 7, WO1: PJ["wo1"] + 7}


def shape_tables():
    import numpy as np
    half = HD // 2
    freqs = (np.float32(10000.0) ** (-np.arange(half, dtype=np.float32) / np.float32(half))).astype(np.float32)
    ang = np.arange(S, dtype=np.float32)[:, None] * freqs[None, :]
    to_rows = lambda a: a.reshape(NT, P, half).transpose(1, 0, 2).reshape(P, NT * half)
    lg = np.log(1.0 - 2.0 ** (-5.0 - np.arange(RET, dtype=np.float64)))
    idx = np.arange(P, dtype=np.float64)
    diff = idx[None, :] - idx[:, None]
    decay = np.where(diff >= 0, np.exp(lg[:, None, None] * np.maximum(diff, 0)), 0.0)
    zeta = np.exp(lg[None, :] * (P - 1 - idx)[:, None])
    xi = np.exp(lg[None, :] * (idx + 1)[:, None])
    dc = np.broadcast_to(np.exp(lg * P)[None, :], (P, RET))
    return np.concatenate([zeta, xi, dc, np.eye(P), to_rows(np.cos(ang)), to_rows(np.sin(ang)),
                           decay.transpose(1, 0, 2).reshape(P, RET * P)], axis=1).astype(np.float32)


_INS = ['x', 'mem', 'w_in', 'b_f', 'w_out', 'w_mem_kv', 'pre_norm', 'post_norm', 'mem_norm']


def kernel(**inputs):
    import numpy as _np
    import concourse.bacc as _bacc
    from concourse import mybir as _mybir
    from concourse.bass_utils import run_bass_kernel_spmd as _run

    nc = _bacc.Bacc("TRN2", target_bir_lowering=False, num_devices=1)
    arrays, args = {}, []
    feed = [(n, _np.ascontiguousarray(inputs[n])) for n in _INS] + [("tables", shape_tables())]
    for name, a in feed:
        arrays[f"in_{name}"] = a
        args.append(nc.dram_tensor(f"in_{name}", a.shape, _mybir.dt.from_np(a.dtype), kind="ExternalInput").ap())
    args.append(nc.dram_tensor("out_0", (1, S, D), _mybir.dt.float32, kind="ExternalOutput").ap())
    build(nc, *args)
    r = _run(nc, [arrays], core_ids=[0])
    return r.results[0]["out_0"]
```

```python
from contextlib import ExitStack

import concourse.bass as bass
from concourse import mybir

F32 = mybir.dt.float32
F16 = mybir.dt.float16
BF16 = mybir.dt.bfloat16
I32 = mybir.dt.int32
ALU = mybir.AluOpType
ACT = mybir.ActivationFunctionType
AX = mybir.AxisListType
RMAX = bass.bass_isa.ReduceOp.max

P = 128
D = 1024
S = 1024
DEPTH = 2
HD = 64
N_MEM = 256
FOX, RET, MEM = 8, 4, 4
EPS = 1e-6
ND = D // P
NT = S // P
NMT = N_MEM // P
HALF = S // 512

FOX_W, RET_W, MEM_W = FOX * HD, RET * HD, MEM * HD
C_FF = 4 * FOX_W
C_RQ = C_FF + FOX
C_RK = C_RQ + RET_W
C_RZ = C_RK + 2 * RET_W
C_MQ = C_RZ + RET_W
C_MZ = C_MQ + MEM_W

FFRQ, RKRV, RZ, MKV, MQ, MZ, FQ, FK, FV, FZ, WO0, WO1 = range(12)
G_PRE, G_MEM, G_ONE = range(3)
CHUNKS = [(FOX + RET_W, C_FF, G_PRE), (2 * RET_W, C_RK, G_PRE), (RET_W, C_RZ, G_PRE), (2 * MEM_W, 0, G_MEM),
          (MEM_W, C_MQ, G_PRE), (MEM_W, C_MZ, G_PRE), (FOX_W, 0, G_PRE), (FOX_W, FOX_W, G_PRE),
          (FOX_W, 2 * FOX_W, G_PRE), (FOX_W, 3 * FOX_W, G_PRE), (512, 0, G_ONE), (512, 512, G_ONE)]
NCH = len(CHUNKS)

_USES = [("ffrq", NT), ("rkrv", NT), ("rz", NT), ("mk", 2), ("mv", NMT), ("mq", 4), ("ma", 2 * MEM),
         ("fq", 8), ("fk", 8), ("fv", NT), ("fa", 2 * FOX), ("wo0", NT), ("wo1", NT)]
PJ = {}
N_PJ = 0
for _n, _c in _USES:
    PJ[_n] = N_PJ
    N_PJ += _c
assert N_PJ % 2 == 0
MZ_U = [PJ["ma"] + 2 * h for h in range(MEM)]
MO_U = [PJ["ma"] + 2 * h + 1 for h in range(MEM)]
FO_U = [PJ["fa"] + 2 * h for h in range(FOX)]
FZ_U = [PJ["fa"] + 2 * h + 1 for h in range(FOX)]

TR_NORM = 0
TR_RET = TR_NORM + 2 * NT
TR_F = TR_RET + 2 * NT
TR_MEM = TR_F + 2
TR_ATT = TR_MEM + 2 * NMT

GRP = 4
ITEMS = [(0, h, t, GRP, NMT) for h in range(MEM) for t in range(0, NT, GRP)] + \
        [(1, h, t, 1, t + 1) for h in range(FOX) for t in range(NT)]
N_MI = MEM * NT // GRP
N_FI = FOX * NT
N_IT = len(ITEMS)
ITEM_TR = []
_u = TR_ATT
for _it in ITEMS:
    ITEM_TR.append(list(range(_u, _u + (_it[3] * _it[4] + 3) // 4)))
    _u += (_it[3] * _it[4] + 3) // 4
TR_Y = _u
N_TR = TR_Y + 2 * NT
assert N_TR % 2 == 0 and N_IT % 2 == 0

CR = 2


def n_full(u):
    return sum(v not in MO_U + FO_U for v in range(u))


N_FULL = n_full(N_PJ)


def n_hi(u):
    return u - min(max(u - TR_RET, 0), TR_MEM - TR_RET)


N_HI = n_hi(N_TR)
SPLIT = [PJ["mk"], PJ["mk"] + 1] + [PJ["mv"] + i for i in range(NMT)] + [PJ["mq"] + i for i in range(4)] + \
        [PJ["fq"] + i for i in range(8)] + [PJ["fk"] + i for i in range(8)] + [PJ["fv"] + i for i in range(NT)]
N_SPLIT = len(SPLIT)
NAT = [(PJ["mk"] + i, 8) for i in range(2)] + [(PJ["mq"] + i, 4) for i in range(4)] + \
      [(PJ["fq"] + i, 4) for i in range(8)] + [(PJ["fk"] + i, 8) for i in range(8)]
NAT_AT = {u: v for v, (u, _) in enumerate(NAT)}
NAT_LAYER = 16 * sum(n for v, (_, n) in enumerate(NAT) if v % 2 == 0)
assert NAT_LAYER == 16 * sum(n for v, (_, n) in enumerate(NAT) if v % 2 == 1)


def nat_count(u):
    v = NAT_AT[u]
    return 16 * sum(n for w, (_, n) in enumerate(NAT) if w <= v and w % 2 == v % 2)


LAG = 5
FFRQ_STEPS = {1: (0, 1), 3: (2, 3), 4: (4, 5, 6)}
RKRV_STEPS = {6: (0,), 7: (1,), 9: (2, 3), 10: (4, 5), 11: (6,)}
FOUR_STEPS = ((0, 1), (2, 3, 4), (5, 6), ())
WO0_AT = [N_MI + NT * (k + 1) + 2 for k in range(7)]
WO1_AT = [N_IT - 4, N_IT - 2]
WO1_STEPS = {1: (2,), 2: (3,), 3: (4,), 4: (5,), 5: (6,)}
FZ_TILES = {2: (0, 2), 3: (2, 4), 4: (4, 5), 5: (5, 6), 6: (6, 7), 7: (7, 8)}

OUT_LAYER = 16 * (NT // 2)
Z_MZ = NT
Z_FZ = Z_MZ + MEM
N_Z = Z_FZ + NT
N_G = 1 + NT
N_SS = NMT + 2 * NT


def build(nc, x, mem, w_in, b_f, w_out, w_mkv, g_pre, g_post, g_mem, tables, out):
    ctx = ExitStack()
    with ctx:
        def sb(name, shape, dt=F32):
            return ctx.enter_context(nc.sbuf_tensor(name, shape, dt))

        def sem(name):
            return ctx.enter_context(nc.semaphore(name))

        hT = sb("hT", [P, 2, ND, S], F16)
        stage = sb("stage", [P, ND, 512])
        wp = sb("wp", [P, 2, 2, ND, 512], F16)
        y = sb("y", [P, NT, D])
        cb = sb("cb", [P, 2, S])
        tp = sb("tp", [P, 3, S])
        pt = sb("pt", [P, 2, 2, S], F16)
        region = sb("region", [P, 16384])
        tab = sb("tab", [P, 140])
        msk = sb("msk", [P, 2, P], BF16)
        fcol = sb("fcol", [P, NT, FOX])
        fabs = sb("fabs", [P, NT, FOX])
        gcol = sb("gcol", [P, 3, ND])
        gabs = sb("gabs", [P, 3, ND])
        bfb = sb("bfb", [P, FOX])
        rmax = sb("rmax", [P, ND])
        pmax = sb("pmax", [P, 1])
        amax = sb("amax", [P, 1])
        sval = sb("sval", [P, NCH])
        unsc = sb("unsc", [P, NCH])
        gs = sb("gs", [P, 2, ND])
        ssq = sb("ssq", [P, N_SS])
        msq = sb("msq", [P, N_SS])
        rstd = sb("rstd", [P, N_SS])
        negh = sb("negh", [P, 4])
        ones1 = sb("ones1", [P, 1])
        gss = sb("gss", [P, NT, 4])
        gms = sb("gms", [P, NT, 4])
        gnr = sb("gnr", [P, NT, 4])
        mxm = sb("mxm", [P, 4, GRP])
        nmm = sb("nmm", [P, 4, GRP])
        sc2 = sb("sc2", [P, 2, 3])
        mx = sb("mx", [P, 4])
        nm = sb("nm", [P, 4])
        rs = sb("rs", [P, 4, NT])
        rec = sb("rec", [P, 4, NT])
        ymax = sb("ymax", [P, NT])
        ysc = sb("ysc", [P, NT])
        yun = sb("yun", [P, NT])
        fo = sb("fo", [P, 2, NT])

        zeta_c, xi_c, dc_c = tab[:, 0:4], tab[:, 4:8], tab[:, 8:12]
        ident = tab[:, 12:140]
        ident_b, mask_b = msk[:, 0, :], msk[:, 1, :]

        def words(a, n, rows=P):
            return region[0:rows, a:a + n]

        xin = words(0, 8192).rearrange("p (t n) -> p t n", t=NT)
        memin = words(14336, 2048).rearrange("p (t n) -> p t n", t=NMT)
        rtab = words(0, 1024)
        cos_t, sin_t, decay_t = rtab[:, 0:256], rtab[:, 256:512], rtab[:, 512:1024]
        memT = words(12288, 2048).bitcast(F16).rearrange("p (a t n) -> p a t n", a=2, t=ND)
        qr = words(2048, 2048).rearrange("p (t n) -> p t n", t=NT)
        kr = words(4096, 512).rearrange("p (a n) -> p a n", a=2)
        kz = words(4608, 512).rearrange("p (a n) -> p a n", a=2)
        rv = words(5120, 512).rearrange("p (a n) -> p a n", a=2)
        rot = words(13056, 512).rearrange("p (a n) -> p a n", a=2)
        qkT = words(6144, 2048, HD).rearrange("p (a b n) -> p a b n", a=2, b=2)
        aT = words(8192, 1024).rearrange("p (a n) -> p a n", a=2)
        rcr = words(9216, 256)
        rsq = words(9472, 256)
        junk = words(9728, 1024)
        state = words(10752, 512, HD).rearrange("p (a n) -> p a n", a=2)
        ro = words(11264, 512).rearrange("p (a n) -> p a n", a=2)
        rst = words(11776, 256, HD)
        crow = words(8192, 1024, FOX)
        mqst = words(13056, 2048).bitcast(F16).rearrange("p (h n) -> p h n", h=MEM)
        mkst = words(15104, 1024).bitcast(F16).rearrange("p (h a n) -> p h a n", h=MEM, a=2)
        mvs = words(9728, 512).bitcast(F16).rearrange("p (a t n) -> p a t n", a=2, t=NMT)
        qst = words(0, 4096).bitcast(F16).rearrange("p (h n) -> p h n", h=FOX)
        kst = words(4096, 8192).bitcast(F16).rearrange("p (h a n) -> p h a n", h=FOX, a=2)
        fvs = words(12288, 4096).bitcast(F16).rearrange("p (a t n) -> p a t n", a=2, t=NT)
        mgate = words(4096, NT * MEM_W).rearrange("p (t n) -> p t n", t=NT)
        fgate = words(4096, NT * FOX_W).rearrange("p (t n) -> p t n", t=NT)
        ost = xin
        gpost = cb[:, 0, :]

        pj = ctx.enter_context(nc.psum_tensor("pj", [P, 2, 512], F32))
        tr = ctx.enter_context(nc.psum_tensor("tr", [P, 2, 512], F32))
        sp = ctx.enter_context(nc.psum_tensor("sp", [P, 2, S], F32))
        ret_a, ret_o, ret_kv = sp[:, 0, 0:512], sp[:, 0, 512:1024], sp[0:HD, 1, 0:256]

        cdram = nc.dram_tensor("c_rows", (FOX, S), F32, kind="Internal").ap()

        held = sem("held")
        tab_in = sem("tab_in")
        w_in_sb = [sem("w_in_sb0"), sem("w_in_sb1")]
        g_in = sem("g_in")
        gp_in = sem("gp_in")
        x_in = [sem(f"x_in{s}") for s in range(NT)]
        mem_in = sem("mem_in")
        rtab_in = sem("rtab_in")
        xr_in = [sem("xr_in0"), sem("xr_in1")]
        st_out = [sem("st_out0"), sem("st_out1")]
        stk_in = [sem("stk_in0"), sem("stk_in1")]
        res_in = [sem("res_in0"), sem("res_in1")]
        c_out = sem("c_out")
        cb_in = [sem("cb_in0"), sem("cb_in1")]
        consts = sem("consts")
        amax_p = sem("amax_p")
        amax_a = sem("amax_a")
        w_scale = sem("w_scale")
        w_hi = sem("w_hi")
        w_half = sem("w_half")
        w_ok = sem("w_ok")
        ss_ok = sem("ss_ok")
        rstd_ok = sem("rstd_ok")
        xh_ok = sem("xh_ok")
        pj_full = sem("pj_full")
        pj_hi = sem("pj_hi")
        pj_free = sem("pj_free")
        silu_ok = sem("silu_ok")
        gate_ok = sem("gate_ok")
        tr_full = sem("tr_full")
        tr_hi = sem("tr_hi")
        tr_free = sem("tr_free")
        kr_ok = sem("kr_ok")
        ra_full = sem("ra_full")
        ra_ok = sem("ra_ok")
        rkv_full = sem("rkv_full")
        state_ok = sem("state_ok")
        ro_full = sem("ro_full")
        ro_free = sem("ro_free")
        gss_ok = sem("gss_ok")
        gnr_ok = sem("gnr_ok")
        fa_ok = sem("fa_ok")
        fl_ok = sem("fl_ok")
        fe_ok = sem("fe_ok")
        lf_ok = sem("lf_ok")
        crow_ok = sem("crow_ok")
        s_full = sem("s_full")
        s_free = sem("s_free")
        mxm_ok = sem("mxm_ok")
        nm_ok = sem("nm_ok")
        p_ok = sem("p_ok")
        pv_done = sem("pv_done")
        ysc_ok = sem("ysc_ok")
        ys_ok = sem("ys_ok")
        o_ok = sem("o_ok")
        out_ok = sem("out_ok")

        def chunk_src(l, c):
            width, c0, _ = CHUNKS[c]
            w = w_mkv if c == MKV else (w_out if c >= WO0 else w_in)
            return w.rearrange("l (p t) n -> l p t n", p=P)[l, :, :, c0:c0 + width]

        x_rows = x.rearrange("b (t p) d -> (b t) p d", p=P)
        mem_rows = mem.rearrange("b (t p) d -> (b t) p d", p=P)
        out_rows = out.rearrange("b (t p) d -> (b t) p d", p=P)

        def norm_rows(j):
            return xin[:, j, :] if j < NT else memin[:, j - NT, :]

        block = ctx.enter_context(nc.Block())

        @block.sync
        def _(q):
            def load_half(l, c, b):
                q.wait_ge(w_ok if b else w_half, l * NCH + c + 1)
                q.sem_inc(held, 1)
                ts = slice(b * ND // 2, (b + 1) * ND // 2)
                q.dma_start(stage[:, ts, 0:CHUNKS[c][0]], chunk_src(l, c)[:, ts, :]).then_inc(w_in_sb[b], 16)

            def load_w(l, c):
                load_half(l, c, 0)
                load_half(l, c, 1)

            def spread(l, u, dst, k_like, head0, s0, n):
                slot = NAT_AT[u] % 2
                q.wait_ge(pj_free, l * N_PJ + u + 1 + CR)
                for b in range(2):
                    rows = slice(HD * b, HD * b + HD)
                    hi, lo = pt[rows, slot, 0, 0:n], pt[rows, slot, 1, 0:n]
                    h = head0 + b
                    if k_like:
                        for a, part in ((0, hi), (1, lo)):
                            for r in range(2):
                                q.dma_start(dst[HD * r:HD * r + HD, h, a, s0:s0 + n], part).then_inc(stk_in[slot], 16)
                    else:
                        q.dma_start(dst[0:HD, h, s0:s0 + n], hi).then_inc(stk_in[slot], 16)
                        q.dma_start(dst[HD:P, h, s0:s0 + n], lo).then_inc(stk_in[slot], 16)

            def load_x(tiles):
                for s in tiles:
                    q.dma_start(xin[:, s, :], x_rows[s]).then_inc(x_in[s], 16)

            def layer(l, first):
                if first:
                    load_x((0,))
                    q.dma_start(tab[:], tables[:, 0:140]).then_inc(tab_in, 16)
                for g, src in ((G_PRE, g_pre), (G_MEM, g_mem)):
                    q.dma_start(gcol[:, g, :], src.rearrange("l (p t) -> l p t", p=P)[l]).then_inc(g_in, 16)
                q.dma_start(bfb[:], b_f[l].partition_broadcast(P)).then_inc(g_in, 16)
                if first:
                    load_x((1,))
                load_w(l, FFRQ)
                if first:
                    load_x(range(2, NT))
                if not first:
                    q.wait_ge(out_ok, l * NT + NT)
                    q.dma_start(out_rows[NT - 1], xin[:, NT - 1, :]).then_inc(st_out[(NT - 1) % 2], 16)
                q.dma_start(memin, mem.rearrange("b (t p) d -> p (b t) d", p=P)).then_inc(mem_in, 16)
                q.wait_ge(tr_free, l * N_TR + 2 + CR)
                q.dma_start(rtab, tables[:, 140:1164]).then_inc(rtab_in, 16)
                load_w(l, RKRV)
                if first:
                    for i in range(2):
                        half = slice(i * NT // 2, (i + 1) * NT // 2)
                        q.dma_start(out_rows[half], x_rows[half]).then_inc(res_in[i], 16)
                load_w(l, RZ)
                load_w(l, MKV)
                load_w(l, MQ)
                for i in range(2):
                    spread(l, PJ["mk"] + i, mkst, True, 2 * i, 0, N_MEM)
                load_w(l, MZ)
                for i in range(4):
                    spread(l, PJ["mq"] + i, mqst, False, 2 * (i // 2), 512 * (i % 2), 512)
                    if i >= 2:
                        load_half(l, FQ, i - 2)
                load_w(l, FK)
                for i in range(8):
                    spread(l, PJ["fq"] + i, qst, False, 2 * (i // 2), 512 * (i % 2), 512)
                    if i in (4, 6):
                        load_half(l, FV, i // 2 - 2)
                q.wait_ge(crow_ok, l + 1)
                q.dma_start(cdram, crow).then_inc(c_out, 16)
                q.wait_ge(c_out, l * 16 + 16)
                for h in range(2):
                    q.dma_start(cb[:, h, :], cdram[h].partition_broadcast(P)).then_inc(cb_in[h], 16)
                for i in range(8):
                    spread(l, PJ["fk"] + i, kst, True, 2 * (i // 2), 512 * (i % 2), 512)
                    if i in (4, 6):
                        load_half(l, FZ, i // 2 - 2)
                load_w(l, WO0)
                for h in range(2, FOX):
                    q.wait_ge(s_free, l * N_FI + NT * (h - 1) + CR)
                    q.dma_start(cb[:, h % 2, :], cdram[h].partition_broadcast(P)).then_inc(cb_in[h % 2], 16)
                load_w(l, WO1)
                q.wait_ge(s_free, l * N_FI + N_FI + CR)
                q.dma_start(gpost, g_post[l].partition_broadcast(P)).then_inc(gp_in, 16)
                q.wait_ge(pj_free, l * N_PJ + PJ["wo0"] + CR)
                q.sem_inc(held, 1)
                for i in range(2):
                    q.wait_ge(res_in[i], 16)
                    q.wait_ge(st_out[i], l * OUT_LAYER + OUT_LAYER)
                    q.sem_inc(held, 1)
                for s in range(2):
                    q.dma_start(tp[:, s, :], out_rows[s]).then_inc(xr_in[s], 16)

            layer(0, True)
            with q.Fori(1, DEPTH) as l:
                layer(l, False)
            q.wait_ge(out_ok, DEPTH * NT + NT)
            q.dma_start(out_rows[NT - 1], xin[:, NT - 1, :]).then_inc(st_out[(NT - 1) % 2], 16)
            for i in range(2):
                q.wait_ge(st_out[i], OUT_LAYER + DEPTH * OUT_LAYER)
            q.wait_ge(c_out, 16 * DEPTH)

        @block.gpsimd
        def _(pool):
            pool.memset(negh[:], -0.5)
            pool.memset(msk[:], 0.0)
            pool.drain()
            pool.affine_select(out=ident_b, in_=ident_b, compare_op=ALU.not_equal, fill=1.0, base=0,
                               pattern=[[-1, P]], channel_multiplier=1)
            pool.affine_select(out=mask_b, in_=mask_b, compare_op=ALU.is_ge, fill=-1e30, base=0,
                               pattern=[[-1, P]], channel_multiplier=1)
            pool.drain()
            pool.memset(ones1[:], 1.0)
            pool.memset(gcol[:, G_ONE, :], 1.0).then_inc(consts, 1)

            def chunk_max(l, c):
                pool.wait_ge(amax_p, l * NCH + c + 1)
                pool.sem_inc(held, 1)
                pool.partition_all_reduce(amax[:], pmax[:], P, RMAX).then_inc(amax_a, 1)

            def inv_rms(l, j):
                pool.wait_ge(ss_ok, l * N_SS + j + 1)
                pool.sem_inc(held, 1)
                pool.tensor_scalar(msq[:, j:j + 1], ssq[:, j:j + 1], 1.0 / D, EPS, ALU.mult, ALU.add)
                pool.drain()
                pool.tensor_tensor(rstd[:, j:j + 1], msq[:, j:j + 1], negh[:, 0:1], ALU.pow).then_inc(rstd_ok, 1)

            pool.wait_ge(consts, 1)
            with pool.Fori(0, DEPTH) as l:
                for j in range(NMT + NT):
                    inv_rms(l, j)
                    if j == 4:
                        chunk_max(l, FFRQ)
                chunk_max(l, RKRV)
                chunk_max(l, RZ)
                for s in range(NT):
                    pool.wait_ge(gss_ok, l * NT + s + 1)
                    pool.sem_inc(held, 1)
                    pool.tensor_scalar(gms[:, s, :], gss[:, s, :], 1.0 / HD, EPS, ALU.mult, ALU.add)
                    pool.drain()
                    pool.tensor_tensor(gnr[:, s, :], gms[:, s, :], negh[:], ALU.pow).then_inc(gnr_ok, 1)
                for c in range(MKV, FQ):
                    chunk_max(l, c)
                for i in range(N_MI):
                    pool.wait_ge(mxm_ok, l * N_MI + i + 1)
                    pool.tensor_tensor(nmm[:, i % 4, :], mxm[:, i % 4, :], sc2[:, 0, 1:2].to_broadcast([P, GRP]),
                                       ALU.mult).then_inc(nm_ok, 1)
                    if i == 1 + 2:
                        chunk_max(l, FQ)
                for c in range(FK, FZ + 1):
                    chunk_max(l, c)
                for i in range(N_MI, N_IT):
                    pool.wait_ge(s_free, l * N_FI + i - N_MI + 1 + CR)
                    pool.tensor_tensor(nm[:, i % 4:i % 4 + 1], mx[:, i % 4:i % 4 + 1], sc2[:, 1, 1:2],
                                       ALU.mult).then_inc(nm_ok, 1)
                    if i == WO0_AT[1] + 2:
                        chunk_max(l, WO0)
                chunk_max(l, WO1)
                for j in range(NMT + NT, N_SS):
                    inv_rms(l, j)

        @block.scalar
        def _(act):
            def prep(l, c, k):
                if not 3 <= k <= 6:
                    return
                width, slot = CHUNKS[c][0], c % 2
                if k == 3:
                    act.wait_ge(w_scale, l * NCH + c + 1)
                    if c >= 2:
                        act.wait_ge(pj_full, l * N_FULL + n_full(LAST[c - 2] + 1))
                for dt in (2 * (k - 3), 2 * (k - 3) + 1):
                    last = act.activation(wp[:, slot, 0, dt, 0:width], stage[:, dt, 0:width], ACT.Copy,
                                          scale=gs[:, slot, dt:dt + 1])
                last.then_inc(w_hi, 1)

            def split_hi(l, u, dst, n):
                act.wait_ge(pj_full, l * N_FULL + n_full(u) + 1)
                if u in NAT_AT and NAT_AT[u] >= 2:
                    prev = NAT[NAT_AT[u] - 2][0]
                    act.wait_ge(stk_in[NAT_AT[u] % 2], l * NAT_LAYER + nat_count(prev))
                act.activation(dst, pj[:, u % 2, 0:n], ACT.Copy).then_inc(pj_hi, 1)

            def tr_split_hi(l, u, dst, shape_t):
                act.wait_ge(tr_full, l * N_TR + u + 1)
                n = shape_t * P
                src = tr[:, u % 2, 0:n]
                if len(dst.shape) == 3:
                    src = src.rearrange("p (t n) -> p t n", t=shape_t)
                act.activation(dst, src, ACT.Copy).then_inc(tr_hi, 1)

            def silu(l, u, c, width):
                act.wait_ge(pj_full, l * N_FULL + n_full(u) + 1)
                act.activation(tp[:, u % 2, 0:width], pj[:, u % 2, 0:width], ACT.Silu,
                               scale=unsc[:, c:c + 1]).then_inc(silu_ok, 1)

            def gates_out(l, u, dst):
                act.wait_ge(pj_full, l * N_FULL + n_full(u) + 1)
                src = pj[:, u % 2, :]
                if len(dst.shape) == 3:
                    src = src.rearrange("p (t n) -> p t n", t=2)
                act.activation(dst, src, ACT.Copy).then_inc(silu_ok, 1)

            def gates_silu(l, z, c, g):
                act.wait_ge(silu_ok, l * N_Z + z + 1)
                act.activation(g, g, ACT.Silu, scale=unsc[:, c:c + 1]).then_inc(gate_ok, 1)

            def attend(l, i0, n_items):
                for i in range(i0, i0 + n_items + 1):
                    if i0 == 0 and i >= 2 and i % 2 == 0:
                        h = i // 2 - 1
                        gates_out(l, MZ_U[h], mgate[:, 2 * h:2 * h + 2, :])
                    if i0 and i - i0 >= 2 * NT and (i - i0) % NT == 0:
                        h = (i - i0) // NT - 2
                        gates_out(l, FZ_U[h], fgate[:, h, :])
                    if i < i0 + n_items:
                        kind, h, t, nt, nk = ITEMS[i]
                        act.wait_ge(nm_ok, l * N_IT + i + 1)
                        n = nk * P
                        for j in range(nt):
                            src = tp[:, i % 3, 0:n] if kind else sp[:, i % 2, j * n:j * n + n]
                            bias = nm[:, i % 4:i % 4 + 1] if kind else nmm[:, i % 4, j:j + 1]
                            last = act.activation(tp[:, i % 3, j * n:j * n + n], src, ACT.Exp, bias=bias,
                                                  scale=sc2[:, kind, 0:1], accum_out=rs[:, h % 4, t + j:t + j + 1])
                        last.then_inc(p_ok, 1)
                    if i > i0:
                        j = i - 1
                        nb = ITEMS[j][3] * ITEMS[j][4]
                        if i == 1:
                            for v in (PJ["mq"] + 2, PJ["mq"] + 3):
                                act.wait_ge(stk_in[NAT_AT[v] % 2], l * NAT_LAYER + nat_count(v))
                                act.sem_inc(held, 1)
                        if j - 2 >= i0:
                            act.wait_ge(pv_done, l * N_IT + j - 1)
                        for b, u in enumerate(ITEM_TR[j]):
                            w = min(4, nb - 4 * b)
                            tr_split_hi(l, u, pt[:, j % 2, 0, 512 * b:512 * b + w * P], w)
                    if i0 == 0:
                        prep(l, FQ, i)
                    elif i in WO0_AT:
                        prep(l, WO0, WO0_AT.index(i))
                    elif i in WO1_AT:
                        prep(l, WO1, WO1_AT.index(i))
                if i0 == 0:
                    gates_silu(l, Z_MZ + MEM - 1, MZ, mgate)

            act.wait_ge(tab_in, 16)
            with act.Fori(0, DEPTH) as l:
                def squares(j):
                    if j < NT:
                        act.wait_ge(x_in[j], 16)
                        act.wait_ge(out_ok, l * NT + j + 1)
                    elif j == NT:
                        act.wait_ge(mem_in, l * 16 + 16)
                    if j >= 1:
                        act.wait_ge(ss_ok, l * N_SS + j)
                    act.activation(junk, norm_rows(j), ACT.Square, accum_out=ssq[:, j:j + 1]).then_inc(ss_ok, 1)

                def store(l, s):
                    act.wait_ge(out_ok, l * NT + s + 1 + NT)
                    act.dma_start(out_rows[s], xin[:, s, :]).then_inc(st_out[s % 2], 16)
                    if s + 2 < NT:
                        act.dma_start(tp[:, s % 2, :], out_rows[s + 2]).then_inc(xr_in[s % 2], 16)

                squares(0)
                squares(1)
                for j in range(NT):
                    squares(j + 2)
                    for b in range(2):
                        tr_split_hi(l, TR_NORM + 2 * j + b, hT[:, 0, 4 * b:4 * b + 4, j * P:j * P + P], 4)
                    for k in FFRQ_STEPS.get(j, ()):
                        prep(l, FFRQ, k)
                for k in range(NT):
                    prep(l, RKRV, k)
                for k in range(NT):
                    prep(l, RZ, k)
                act.wait_ge(fa_ok, l + 1)
                act.activation(fabs[:], fabs[:], ACT.Exp, scale=-1.0).then_inc(fe_ok, 1)
                act.wait_ge(fe_ok, l + 1)
                act.activation(fabs[:], fabs[:], ACT.Ln, bias=1.0).then_inc(fl_ok, 1)
                for s in range(NT):
                    silu(l, PJ["rz"] + s, RZ, RET_W)
                    prep(l, MKV, s)
                    if 2 <= s < 2 + NMT:
                        for b in range(2):
                            tr_split_hi(l, TR_MEM + 2 * (s - 2) + b,
                                        memT[:, 0, 4 * b:4 * b + 4, (s - 2) * P:(s - 1) * P], 4)
                for i in range(2 + NMT):
                    u = PJ["mk"] + i
                    if i < 2:
                        split_hi(l, u, pt[:, NAT_AT[u] % 2, 0, 0:N_MEM], N_MEM)
                    else:
                        split_hi(l, u, mvs[:, 0, i - 2, :], MEM_W)
                    for k in FOUR_STEPS[i]:
                        prep(l, MQ, k)
                for i in range(4):
                    u = PJ["mq"] + i
                    split_hi(l, u, pt[:, NAT_AT[u] % 2, 0, 0:512], 512)
                    for k in FOUR_STEPS[i]:
                        prep(l, MZ, k)
                attend(l, 0, N_MI)
                for i in range(8):
                    u = PJ["fq"] + i
                    split_hi(l, u, pt[:, NAT_AT[u] % 2, 0, 0:512], 512)
                    prep(l, FK, i)
                for i in range(8):
                    u = PJ["fk"] + i
                    split_hi(l, u, pt[:, NAT_AT[u] % 2, 0, 0:512], 512)
                    prep(l, FV, i)
                for s in range(NT):
                    split_hi(l, PJ["fv"] + s, fvs[:, 0, s, :], FOX_W)
                    prep(l, FZ, s)
                attend(l, N_MI, N_IT - N_MI)
                for s in range(-2, NT + 1):
                    if 1 <= s <= NT:
                        for b in range(2):
                            tr_split_hi(l, TR_Y + 2 * (s - 1) + b, hT[:, 0, 4 * b:4 * b + 4, (s - 1) * P:s * P], 4)
                    for k in WO1_STEPS.get(s, ()):
                        prep(l, WO1, k)
                    if 0 <= s < NT:
                        act.wait_ge(ysc_ok, l * NT + s + 1)
                        act.activation(y[:, s, :], y[:, s, :], ACT.Copy, scale=ysc[:, s:s + 1]).then_inc(ys_ok, 1)
                    if s == 1:
                        gates_out(l, FZ_U[FOX - 1], fgate[:, FOX - 1, :])
                    if s + 2 < NT:
                        gates_silu(l, Z_FZ + s + 2, FZ, fgate[:, s + 2, :])
                for s in range(NT):
                    j = NMT + NT + s
                    act.wait_ge(o_ok, l * NT + s + 1)
                    act.wait_ge(ss_ok, l * N_SS + j)
                    act.activation(words(8192, 1024), ost[:, s, :], ACT.Square,
                                   accum_out=ssq[:, j:j + 1]).then_inc(ss_ok, 1)
                    if s >= 1:
                        store(l, s - 1)

        @block.tensor
        def _(pe):
            def open_unit(l, u):
                pe.wait_ge(pj_free, l * N_PJ + u + 1)

            def rows_unit(l, u, c, lhs, t, c0, n, tiles=(0, ND)):
                if tiles[0] == 0:
                    open_unit(l, u)
                for dt in range(*tiles):
                    for a, b in ((0, 0), (0, 1), (1, 0)):
                        last = pe.matmul(pj[:, u % 2, 0:n], lhs[:, a, dt, t * P:t * P + P],
                                         wp[:, c % 2, b, dt, c0:c0 + n],
                                         start=(dt == 0 and a + b == 0), stop=(dt == ND - 1 and a == 1))
                if tiles[1] == ND:
                    last.then_inc(pj_full, 1)

            def cols_unit(l, u, c, rhs, e0, s0, n):
                open_unit(l, u)
                for dt in range(ND):
                    for a, b in ((0, 0), (0, 1), (1, 0)):
                        last = pe.matmul(pj[:, u % 2, 0:n], wp[:, c % 2, a, dt, e0:e0 + P],
                                         rhs[:, b, dt, s0:s0 + n],
                                         start=(dt == 0 and a + b == 0), stop=(dt == ND - 1 and a == 1))
                last.then_inc(pj_full, 1)

            def chunk_ready(l, c):
                pe.wait_ge(w_ok, l * NCH + c + 2)

            def transposes(l, u, srcs, rows=P):
                pe.wait_ge(tr_free, l * N_TR + u + 1)
                if rows != P:
                    pe.sem_inc(held, 1)
                for k, src in enumerate(srcs):
                    last = pe.transpose(tr[0:rows, u % 2, k * P:k * P + P], src, ident)
                last.then_inc(tr_full, 1)

            def ret_out(l, s):
                pe.wait_ge(ra_ok, l * NT + s + 1)
                if s > 0:
                    pe.wait_ge(state_ok, l * NT + s)
                    pe.wait_ge(ro_free, l * NT + s)
                r = s % 2
                for h in range(RET):
                    e = slice(h * HD, h * HD + HD)
                    last = pe.matmul(ret_o[:, e], aT[:, r, h * P:h * P + P], rv[:, r, e], start=True, stop=True)
                if s > 0:
                    for h in range(RET):
                        e = slice(h * HD, h * HD + HD)
                        last = pe.matmul(ret_o[:, 256 + h * HD:256 + h * HD + HD], qkT[:, r, 0, h * P:h * P + P],
                                         state[:, r, e], start=True, stop=True)
                last.then_inc(ro_full, 1)

            def ret_transposes(l, s):
                pe.wait_ge(kr_ok, l * NT + s + 1)
                transposes(l, TR_RET + 2 * s, [qr[:, s, h * HD:h * HD + HD] for h in range(RET)], HD)
                transposes(l, TR_RET + 2 * s + 1, [kr[:, s % 2, h * HD:h * HD + HD] for h in range(RET)], HD)

            def ret_scores(l, s):
                r = s % 2
                pe.wait_ge(tr_free, l * N_TR + TR_RET + 2 * s + 2 + CR)
                for h in range(RET):
                    last = pe.matmul(ret_a[:, h * P:h * P + P], qkT[:, r, 1, h * P:h * P + P],
                                     qkT[:, r, 0, h * P:h * P + P], start=True, stop=True)
                last.then_inc(ra_full, 1)
                if s > 0:
                    pe.wait_ge(state_ok, l * NT + s)
                for h in range(RET):
                    e = slice(h * HD, h * HD + HD)
                    last = pe.matmul(ret_kv[:, e], kz[:, r, e], rv[:, r, e], start=True, stop=True)
                last.then_inc(rkv_full, 1)

            def stacks_in(l, u):
                for v in (u, u + 1):
                    pe.wait_ge(stk_in[NAT_AT[v] % 2], l * NAT_LAYER + nat_count(v))

            def item_scores(l, i):
                kind, h, t, nt, nk = ITEMS[i]
                if (kind, h, t) == (0, 2, 0):
                    stacks_in(l, PJ["mq"] + 2)
                    pe.sem_inc(held, 1)
                if kind:
                    pe.wait_ge(s_free, l * N_FI + i - N_MI + 1)
                elif i >= 2:
                    pe.wait_ge(p_ok, l * N_IT + i - 1)
                k = kst if kind else mkst
                for j in range(nt):
                    q = (qst if kind else mqst)[:, h, (t + j) * P:(t + j + 1) * P]
                    for a in range(0, nk * P, 512):
                        n = min(512, nk * P - a)
                        c0 = j * nk * P + a
                        o = sp[:, i % 2, c0:c0 + n]
                        diag = kind and a + n == nk * P
                        pe.matmul(o, q, k[:, h, 0, a:a + n], start=True, stop=False)
                        last = pe.matmul(o, q, k[:, h, 1, a:a + n], start=False, stop=not diag)
                        if diag:
                            last = pe.matmul(sp[:, i % 2, a + n - P:a + n], ident_b, mask_b, start=False, stop=True)
                last.then_inc(s_full, 1)

            def item_transposes(l, i):
                pe.wait_ge(p_ok, l * N_IT + i + 1)
                nb = ITEMS[i][3] * ITEMS[i][4]
                for b, u in enumerate(ITEM_TR[i]):
                    transposes(l, u, [tp[:, i % 3, k * P:k * P + P] for k in range(4 * b, min(nb, 4 * b + 4))])

            def item_values(l, i):
                kind, h, t, nt, nk = ITEMS[i]
                u = (FO_U if kind else MO_U)[h]
                if t == 0:
                    open_unit(l, u)
                pe.wait_ge(tr_free, l * N_TR + ITEM_TR[i][-1] + 1 + CR)
                v = fvs if kind else mvs
                e = slice(h * HD, h * HD + HD)
                for j in range(nt):
                    o = pj[:, u % 2, (t + j) * HD:(t + j + 1) * HD]
                    for k in range(nk):
                        p0 = (j * nk + k) * P
                        for a, b in ((0, 0), (0, 1), (1, 0)):
                            last = pe.matmul(o, pt[:, i % 2, a, p0:p0 + P], v[:, b, k, e],
                                             start=(k == 0 and a + b == 0), stop=(k == nk - 1 and a == 1))
                last.then_inc(pv_done, 1)

            def attend(l, i0, n_items):
                end = i0 + n_items
                item_scores(l, i0)
                item_scores(l, i0 + 1)
                for i in range(i0, end + 2):
                    if i0 == 0 and i < end and i != 1:
                        if i == 0:
                            mz_half(l, 0, 0)
                        mz_half(l, i // 2, 1 if i == 0 else i % 2)
                    if i + 2 < end:
                        item_scores(l, i + 2)
                    if i0 and i < end and ITEMS[i][1] >= 1:
                        h, t = ITEMS[i][1:3]
                        if t in FZ_TILES:
                            rows_unit(l, FZ_U[h - 1], FZ, hT, h - 1, 0, FOX_W, FZ_TILES[t])
                    if i0 <= i - 2:
                        item_values(l, i - 2)
                    if i < end:
                        item_transposes(l, i)
                    if i == end:
                        if i0 == 0:
                            chunk_ready(l, FQ)
                            cols_unit(l, PJ["fq"], FQ, hT, 0, 0, 512)
                        else:
                            last_gates(l, 0, 3)
                if i0:
                    last_gates(l, 3, 5)

            def last_gates(l, a, b):
                rows_unit(l, FZ_U[FOX - 1], FZ, hT, FOX - 1, 0, FOX_W, (a, b))

            def mz_half(l, h, b):
                u = MZ_U[h]
                if b == 0:
                    open_unit(l, u)
                t = 2 * h + b
                for dt in range(ND):
                    for a, w in ((0, 0), (0, 1), (1, 0)):
                        last = pe.matmul(pj[:, u % 2, b * MEM_W:(b + 1) * MEM_W], hT[:, a, dt, t * P:t * P + P],
                                         wp[:, MZ % 2, w, dt, 0:MEM_W], start=(dt == 0 and a + w == 0),
                                         stop=(dt == ND - 1 and a == 1))
                if b == 1:
                    last.then_inc(pj_full, 1)

            pe.wait_ge(consts, 1)
            pe.wait_ge(tab_in, 16)
            with pe.Fori(0, DEPTH) as l:
                def norm_transposes(j, u):
                    pe.wait_ge(xh_ok, l * (NMT + NT) + j + 1)
                    for b in range(2):
                        transposes(l, u + b, [norm_rows(j)[:, k:D:ND] for k in range(4 * b, 4 * b + 4)])

                for j in range(NT + LAG):
                    if j < NT:
                        norm_transposes(j, TR_NORM + 2 * j)
                    if j == LAG:
                        chunk_ready(l, FFRQ)
                    if j >= LAG:
                        s = j - LAG
                        pe.wait_ge(tr_free, l * N_TR + TR_NORM + 2 * s + 2 + CR)
                        rows_unit(l, PJ["ffrq"] + s, FFRQ, hT, s, 0, FOX + RET_W)
                chunk_ready(l, RKRV)
                for s in range(NT + 2):
                    if s < NT:
                        rows_unit(l, PJ["rkrv"] + s, RKRV, hT, s, 0, 2 * RET_W, (0, ND // 2))
                    if 1 <= s <= NT:
                        ret_transposes(l, s - 1)
                    if s >= 2:
                        ret_out(l, s - 2)
                    if s < NT:
                        rows_unit(l, PJ["rkrv"] + s, RKRV, hT, s, 0, 2 * RET_W, (ND // 2, ND))
                    if 1 <= s <= NT:
                        ret_scores(l, s - 1)
                pe.wait_ge(lf_ok, l + 1)
                for b in range(2):
                    transposes(l, TR_F + b, [fcol[:, s, :] for s in range(4 * b, 4 * b + 4)], FOX)
                chunk_ready(l, RZ)
                for s in range(NT):
                    rows_unit(l, PJ["rz"] + s, RZ, hT, s, 0, RET_W)
                    if 2 <= s < 2 + NMT:
                        norm_transposes(NT + s - 2, TR_MEM + 2 * (s - 2))
                pe.wait_ge(tr_free, l * N_TR + TR_ATT + CR)
                chunk_ready(l, MKV)
                for i in range(2):
                    cols_unit(l, PJ["mk"] + i, MKV, memT, i * P, 0, N_MEM)
                for i in range(NMT):
                    rows_unit(l, PJ["mv"] + i, MKV, memT, i, MEM_W, MEM_W)
                chunk_ready(l, MQ)
                for i in range(4):
                    cols_unit(l, PJ["mq"] + i, MQ, hT, (i // 2) * P, 512 * (i % 2), 512)
                chunk_ready(l, MZ)
                stacks_in(l, PJ["mq"])
                attend(l, 0, N_MI)
                for i in range(1, 8):
                    cols_unit(l, PJ["fq"] + i, FQ, hT, (i // 2) * P, 512 * (i % 2), 512)
                chunk_ready(l, FK)
                for i in range(8):
                    cols_unit(l, PJ["fk"] + i, FK, hT, (i // 2) * P, 512 * (i % 2), 512)
                chunk_ready(l, FV)
                for s in range(NT):
                    rows_unit(l, PJ["fv"] + s, FV, hT, s, 0, FOX_W)
                for b in range(2):
                    pe.wait_ge(stk_in[b], l * NAT_LAYER + NAT_LAYER)
                chunk_ready(l, FZ)
                attend(l, N_MI, N_IT - N_MI)
                chunk_ready(l, WO0)
                for s in range(NT + 1):
                    if s < NT:
                        pe.wait_ge(ys_ok, l * NT + s + 1)
                        for b in range(2):
                            transposes(l, TR_Y + 2 * s + b, [y[:, s, k:D:ND] for k in range(4 * b, 4 * b + 4)])
                    if s == 0:
                        last_gates(l, 5, ND)
                    if s >= 1:
                        pe.wait_ge(tr_free, l * N_TR + TR_Y + 2 * s + CR)
                        rows_unit(l, PJ["wo0"] + s - 1, WO0, hT, s - 1, 0, 512)
                chunk_ready(l, WO1)
                for s in range(NT):
                    rows_unit(l, PJ["wo1"] + s, WO1, hT, s, 0, 512)

        @block.vector
        def _(dve):
            def prep(l, c, k):
                width, _, g = CHUNKS[c]
                slot = c % 2
                if 0 <= k < 2:
                    dve.wait_ge(w_in_sb[k], l * 16 * NCH + 16 * c + 16)
                    dve.tensor_reduce(rmax[:, 4 * k:4 * k + 4], stage[:, 4 * k:4 * k + 4, 0:width], AX.X, ALU.max,
                                      apply_absolute_value=True)
                if k == 1:
                    dve.drain()
                    dve.tensor_tensor(rmax[:], rmax[:], gabs[:, g, :], ALU.mult)
                    dve.drain()
                    dve.tensor_reduce(pmax[:], rmax[:], AX.X, ALU.max).then_inc(amax_p, 1)
                if k == 2:
                    dve.wait_ge(amax_a, l * NCH + c + 1)
                    dve.tensor_scalar(amax[:], amax[:], 2.0 ** -30, None, ALU.max)
                    dve.drain()
                    power_of_two(sval[:, c:c + 1], unsc[:, c:c + 1], amax[:])
                    dve.tensor_scalar(gs[:, slot, :], gcol[:, g, :], sval[:, c:c + 1], None,
                                      ALU.mult).then_inc(w_scale, 1)
                if 3 <= k <= 6:
                    if k == 3:
                        dve.drain()
                    dve.wait_ge(w_hi, l * 4 * NCH + 4 * c + k - 2)
                    for dt in (2 * (k - 3), 2 * (k - 3) + 1):
                        last = dve.scalar_tensor_tensor(wp[:, slot, 1, dt, 0:width], stage[:, dt, 0:width],
                                                        gs[:, slot, dt:dt + 1], wp[:, slot, 0, dt, 0:width],
                                                        ALU.mult, ALU.subtract)
                    if k == 4:
                        last.then_inc(w_half, 1)
                    if k == 6:
                        last.then_inc(w_ok, 1)

            def power_of_two(up, down, m):
                dve.tensor_scalar(down.bitcast(I32), m.bitcast(I32), 0x7F800000, None, ALU.bitwise_and)
                dve.drain()
                dve.tensor_scalar(up.bitcast(I32), down.bitcast(I32), -1.0, float(0x7F000000), ALU.mult, ALU.add)
                dve.drain()

            def split_lo(l, u, hi, lo, n):
                dve.wait_ge(pj_hi, l * N_SPLIT + SPLIT.index(u) + 1)
                dve.tensor_tensor(lo, pj[:, u % 2, 0:n], hi, ALU.subtract).then_inc(pj_free, 1)

            def tr_split_lo(l, u, hi, lo, w):
                dve.wait_ge(tr_hi, l * N_HI + n_hi(u) + 1)
                src = tr[:, u % 2, 0:w * P]
                if len(hi.shape) == 3:
                    src = src.rearrange("p (t n) -> p t n", t=w)
                dve.tensor_tensor(lo, src, hi, ALU.subtract).then_inc(tr_free, 1)

            def gate(l, u, z, s, c0, width):
                dve.wait_ge(silu_ok, l * N_Z + z + 1)
                yv = y[:, s, c0:c0 + width]
                dve.tensor_tensor(yv, yv, tp[:, u % 2, 0:width], ALU.mult).then_inc(pj_free, 1)

            def rotary(src, s, scale):
                cos_now = cos_t[:, 32 * s:32 * s + 32].unsqueeze(1).to_broadcast([P, 2 * RET, 32])
                sin_now = sin_t[:, 32 * s:32 * s + 32].unsqueeze(1).to_broadcast([P, 2 * RET, 32])
                s8 = src.rearrange("p (h j) -> p h j", j=32)
                dve.scalar_tensor_tensor(rot[:, 0, :].rearrange("p (h j) -> p h j", j=32), s8, scale, cos_now,
                                         ALU.mult, ALU.mult)
                last = dve.scalar_tensor_tensor(rot[:, 1, :].rearrange("p (h j) -> p h j", j=32), s8, scale, sin_now,
                                                ALU.mult, ALU.mult)
                return last

            def rotary_sum(dst):
                t1 = rot[:, 0, :].rearrange("p (h two j) -> p h two j", two=2, j=32)
                t2 = rot[:, 1, :].rearrange("p (h two j) -> p h two j", two=2, j=32)
                d = dst.rearrange("p (h two j) -> p h two j", two=2, j=32)
                dve.tensor_tensor(d[:, :, 0, :], t1[:, :, 0, :], t2[:, :, 1, :], ALU.subtract)
                return dve.tensor_tensor(d[:, :, 1, :], t1[:, :, 1, :], t2[:, :, 0, :], ALU.add)

            def heads(ap):
                return ap.rearrange("p (h e) -> p h e", h=RET)

            def over_head(col, n=P):
                return col.unsqueeze(2).to_broadcast([n, RET, HD])

            def item_max(l, i, i0):
                kind, h, t, nt, nk = ITEMS[i]
                n = nk * P
                dve.wait_ge(s_full, l * N_IT + i + 1)
                if not kind:
                    dve.tensor_reduce(mxm[:, i % 4, :], sp[:, i % 2, :].rearrange("p (t n) -> p t n", t=nt), AX.X,
                                      ALU.max).then_inc(mxm_ok, 1)
                    return
                if i - 3 >= i0:
                    dve.wait_ge(tr_full, l * N_TR + ITEM_TR[i - 3][-1] + 1)
                if t == 0:
                    dve.wait_ge(cb_in[h % 2], l * 16 * (FOX // 2) + 16 * (h // 2) + 16)
                dve.sem_inc(held, 1)
                dve.tensor_tensor_reduce(tp[:, i % 3, 0:n], sp[:, i % 2, 0:n], cb[:, h % 2, 0:n], 1.0, -3.0e38, ALU.add, ALU.max,
                                         mx[:, i % 4:i % 4 + 1]).then_inc(s_free, 1)

            def head_out(l, i):
                kind, h = ITEMS[i][0:2]
                u = (FO_U if kind else MO_U)[h]
                c = FV if kind else MKV
                c0 = (0 if kind else FOX_W + RET_W) + h * HD
                r = h % 4
                dve.wait_ge(pv_done, l * N_IT + i + 1)
                dve.reciprocal(rec[:, r, :], rs[:, r, :])
                dve.drain()
                dve.tensor_scalar(rec[:, r, :], rec[:, r, :], unsc[:, c:c + 1], None, ALU.mult)
                dve.drain()
                dve.tensor_tensor(y[:, :, c0:c0 + HD], pj[:, u % 2, :].rearrange("p (t e) -> p t e", t=NT),
                                  rec[:, r, :].unsqueeze(2).to_broadcast([P, NT, HD]), ALU.mult).then_inc(pj_free, 1)

            def gate_out(l, z):
                dve.drain()
                dve.wait_ge(silu_ok, l * N_Z + z + 1)
                dve.sem_inc(pj_free, 1)

            def attend(l, i0, n_items):
                end = i0 + n_items
                item_max(l, i0, i0)
                item_max(l, i0 + 1, i0)
                for i in range(i0, end + 2):
                    if i0 and 2 * NT <= i - i0 and (i - i0) % NT == 0:
                        gate_out(l, Z_FZ + (i - i0) // NT - 2)
                    j = i - 1
                    if i0 <= j < end:
                        nb = ITEMS[j][3] * ITEMS[j][4]
                        for b, u in enumerate(ITEM_TR[j]):
                            w = min(4, nb - 4 * b)
                            sl = slice(512 * b, 512 * b + w * P)
                            tr_split_lo(l, u, pt[:, j % 2, 0, sl], pt[:, j % 2, 1, sl], w)
                    if i + 2 < end:
                        item_max(l, i + 2, i0)
                    if i0 <= i - 2 and ITEMS[i - 2][2] + ITEMS[i - 2][3] == NT:
                        head_out(l, i - 2)
                    if i0 == 0 and i < end and i % 2:
                        gate_out(l, Z_MZ + i // 2)
                    if i0 == 0:
                        prep(l, FQ, i)
                    elif i in WO0_AT:
                        prep(l, WO0, WO0_AT.index(i))
                    elif i in WO1_AT:
                        prep(l, WO1, WO1_AT.index(i))
                dve.drain()

            def attention_scale(kind, cq, ck):
                dve.tensor_scalar(sc2[:, kind, 0:1], unsc[:, cq:cq + 1], unsc[:, ck:ck + 1], HD ** -0.5,
                                  ALU.mult, ALU.mult)
                dve.tensor_scalar(sc2[:, kind, 2:3], sval[:, cq:cq + 1], sval[:, ck:ck + 1], -(HD ** 0.5),
                                  ALU.mult, ALU.mult)
                dve.drain()
                dve.tensor_scalar(sc2[:, kind, 1:2], sc2[:, kind, 0:1], -1.0, None, ALU.mult)
                dve.drain()

            dve.wait_ge(consts, 1)
            dve.sem_inc(pj_free, CR)
            dve.sem_inc(tr_free, CR)
            dve.sem_inc(s_free, CR)
            dve.sem_inc(w_half, 1)
            dve.sem_inc(w_ok, 1)
            dve.sem_inc(out_ok, NT)
            for i in range(2):
                dve.sem_inc(st_out[i], OUT_LAYER)
            dve.wait_ge(tab_in, 16)
            with dve.Fori(0, DEPTH) as l:
                def norm(j):
                    dve.wait_ge(rstd_ok, l * N_SS + j + 1)
                    if j < NT:
                        dve.wait_ge(st_out[j % 2], l * OUT_LAYER + 16 * (j // 2) + 16)
                    dve.tensor_scalar(norm_rows(j), norm_rows(j), rstd[:, j:j + 1], None, ALU.mult).then_inc(xh_ok, 1)

                def ffrq_out(s):
                    u = PJ["ffrq"] + s
                    dve.drain()
                    dve.wait_ge(pj_full, l * N_FULL + n_full(u) + 1)
                    dve.scalar_tensor_tensor(fcol[:, s, :], pj[:, u % 2, 0:FOX], unsc[:, FFRQ:FFRQ + 1], bfb[:],
                                             ALU.mult, ALU.add)
                    rotary(pj[:, u % 2, FOX:FOX + RET_W], s, unsc[:, FFRQ:FFRQ + 1]).then_inc(pj_free, 1)
                    dve.drain()
                    rotary_sum(qr[:, s, :])

                norm(0)
                for j in range(NT + LAG):
                    if j + 1 < NT:
                        norm(j + 1)
                    if j < NT:
                        for b in range(2):
                            cs = slice(j * P, j * P + P)
                            tr_split_lo(l, TR_NORM + 2 * j + b, hT[:, 0, 4 * b:4 * b + 4, cs],
                                        hT[:, 1, 4 * b:4 * b + 4, cs], 4)
                    if j == 1:
                        dve.wait_ge(g_in, l * 48 + 48)
                        dve.scalar_tensor_tensor(gabs[:], gcol[:], -1.0, gcol[:], ALU.mult, ALU.max)
                    for k in FFRQ_STEPS.get(j, ()):
                        prep(l, FFRQ, k)
                    if j == LAG:
                        dve.wait_ge(rtab_in, l * 16 + 16)
                        dve.sem_inc(held, 1)
                    if j >= LAG:
                        ffrq_out(j - LAG)
                    for k in RKRV_STEPS.get(j, ()):
                        prep(l, RKRV, k)
                dve.drain()
                dve.scalar_tensor_tensor(fabs[:], fcol[:], -1.0, fcol[:], ALU.mult, ALU.max).then_inc(fa_ok, 1)
                dve.tensor_scalar(sc2[:, 0, 0:1], unsc[:, RKRV:RKRV + 1], HD ** -0.5, None, ALU.mult)
                dve.drain()
                for s in range(NT + 3):
                    if 1 <= s <= NT:
                        n = s - 1
                        r = n % 2
                        for b in range(2):
                            u = TR_RET + 2 * n + b
                            dve.wait_ge(tr_full, l * N_TR + u + 1)
                            dve.tensor_copy(qkT[:, r, b, :], tr[0:HD, u % 2, :]).then_inc(tr_free, 1)
                    if 2 <= s < NT + 2:
                        n = s - 2
                        r = n % 2
                        dve.wait_ge(ro_full, l * NT + n + 1)
                        if n == 0:
                            dve.tensor_copy(ro[:, r, :], ret_o[:, 0:256]).then_inc(ro_free, 1)
                        else:
                            dve.tensor_tensor(heads(rcr), heads(ret_o[:, 256:512]), over_head(xi_c), ALU.mult)
                            dve.drain()
                            dve.tensor_tensor(ro[:, r, :], ret_o[:, 0:256], rcr, ALU.add).then_inc(ro_free, 1)
                        dve.drain()
                        dve.tensor_tensor(rsq, ro[:, r, :], ro[:, r, :], ALU.mult)
                        dve.drain()
                        dve.tensor_reduce(gss[:, n, :], heads(rsq), AX.X, ALU.add).then_inc(gss_ok, 1)
                    if s < NT:
                        u = PJ["rkrv"] + s
                        r = s % 2
                        dve.drain()
                        dve.wait_ge(pj_full, l * N_FULL + n_full(u) + 1)
                        rotary(pj[:, u % 2, 0:RET_W], s, sc2[:, 0, 0:1])
                        dve.tensor_scalar(rv[:, r, :], pj[:, u % 2, RET_W:2 * RET_W], unsc[:, RKRV:RKRV + 1], None,
                                          ALU.mult).then_inc(pj_free, 1)
                        dve.drain()
                        rotary_sum(kr[:, r, :])
                        dve.drain()
                        dve.tensor_tensor(heads(kz[:, r, :]), heads(kr[:, r, :]), over_head(zeta_c),
                                          ALU.mult).then_inc(kr_ok, 1)
                    if s >= 3:
                        n = s - 3
                        dve.wait_ge(gnr_ok, l * NT + n + 1)
                        dve.tensor_tensor(heads(y[:, n, FOX_W:FOX_W + RET_W]), heads(ro[:, n % 2, :]),
                                          over_head(gnr[:, n, :]), ALU.mult)
                    if 1 <= s <= NT:
                        n = s - 1
                        r = n % 2
                        dve.wait_ge(ra_full, l * NT + n + 1)
                        dve.tensor_tensor(aT[:, r, :], ret_a, decay_t, ALU.mult).then_inc(ra_ok, 1)
                        dve.wait_ge(rkv_full, l * NT + n + 1)
                        if n == 0:
                            dve.tensor_copy(state[:, 1, :], ret_kv).then_inc(state_ok, 1)
                        else:
                            dve.tensor_tensor(heads(rst), heads(state[:, r, :]), over_head(dc_c[0:HD, :], HD),
                                              ALU.mult)
                            dve.drain()
                            dve.tensor_tensor(state[:, 1 - r, :], rst, ret_kv, ALU.add).then_inc(state_ok, 1)
                    if s < NT:
                        prep(l, RZ, s)
                dve.wait_ge(fl_ok, l + 1)
                dve.scalar_tensor_tensor(fcol[:], fcol[:], 0.0, fabs[:], ALU.min, ALU.subtract).then_inc(lf_ok, 1)
                for b in range(2):
                    u = TR_F + b
                    dve.wait_ge(tr_full, l * N_TR + u + 1)
                    dve.tensor_tensor_scan(crow[:, 512 * b:512 * b + 512],
                                           ones1[0:FOX, :].to_broadcast([FOX, 512]), tr[0:FOX, u % 2, :],
                                           crow[:, 511:512] if b else 0.0, ALU.mult, ALU.add).then_inc(tr_free, 1)
                    dve.drain()
                norm(NT)
                norm(NT + 1)
                for s in range(NT):
                    gate(l, PJ["rz"] + s, s, s, FOX_W, RET_W)
                    prep(l, MKV, s)
                    if 2 <= s < 2 + NMT:
                        cs = slice((s - 2) * P, (s - 1) * P)
                        for b in range(2):
                            tr_split_lo(l, TR_MEM + 2 * (s - 2) + b, memT[:, 0, 4 * b:4 * b + 4, cs],
                                        memT[:, 1, 4 * b:4 * b + 4, cs], 4)
                for i in range(2 + NMT):
                    u = PJ["mk"] + i
                    if i < 2:
                        sl = NAT_AT[u] % 2
                        split_lo(l, u, pt[:, sl, 0, 0:N_MEM], pt[:, sl, 1, 0:N_MEM], N_MEM)
                    else:
                        split_lo(l, u, mvs[:, 0, i - 2, :], mvs[:, 1, i - 2, :], MEM_W)
                    for k in FOUR_STEPS[i]:
                        prep(l, MQ, k)
                for i in range(4):
                    sl = NAT_AT[PJ["mq"] + i] % 2
                    split_lo(l, PJ["mq"] + i, pt[:, sl, 0, 0:512], pt[:, sl, 1, 0:512], 512)
                    for k in FOUR_STEPS[i]:
                        prep(l, MZ, k)
                attention_scale(0, MQ, MKV)
                attend(l, 0, N_MI)
                ym = y[:, :, FOX_W + RET_W:D]
                for i in range(8):
                    sl = NAT_AT[PJ["fq"] + i] % 2
                    split_lo(l, PJ["fq"] + i, pt[:, sl, 0, 0:512], pt[:, sl, 1, 0:512], 512)
                    if i == 1:
                        dve.wait_ge(gate_ok, l * N_G + 1)
                        dve.tensor_tensor(ym, ym, mgate, ALU.mult)
                    prep(l, FK, i)
                attention_scale(1, FQ, FK)
                dve.tensor_scalar(crow, crow, sc2[0:FOX, 1, 2:3], None, ALU.mult).then_inc(crow_ok, 1)
                for i in range(8):
                    sl = NAT_AT[PJ["fk"] + i] % 2
                    split_lo(l, PJ["fk"] + i, pt[:, sl, 0, 0:512], pt[:, sl, 1, 0:512], 512)
                    prep(l, FV, i)
                for s in range(NT):
                    split_lo(l, PJ["fv"] + s, fvs[:, 0, s, :], fvs[:, 1, s, :], 512)
                    prep(l, FZ, s)
                attend(l, N_MI, N_IT - N_MI)
                for s in range(NT + 2):
                    if s < NT:
                        one = slice(s, s + 1)
                        yv = y[:, s, 0:FOX_W]
                        dve.wait_ge(gate_ok, l * N_G + s + 2)
                        dve.tensor_tensor(yv, yv, fgate[:, s, :], ALU.mult)
                        dve.drain()
                        dve.tensor_reduce(ymax[:, one], y[:, s, :], AX.X, ALU.max, apply_absolute_value=True)
                        dve.drain()
                        dve.tensor_scalar(ymax[:, one], ymax[:, one], 2.0 ** -30, None, ALU.max)
                        dve.drain()
                        power_of_two(ysc[:, one], yun[:, one], ymax[:, one])
                        dve.tensor_scalar(fo[:, 0, one], yun[:, one], unsc[:, WO0:WO0 + 1], None,
                                          ALU.mult).then_inc(ysc_ok, 1)
                    if s == 1:
                        gate_out(l, Z_FZ + FOX - 1)
                    if 1 <= s <= NT:
                        for b in range(2):
                            cs = slice((s - 1) * P, s * P)
                            tr_split_lo(l, TR_Y + 2 * (s - 1) + b, hT[:, 0, 4 * b:4 * b + 4, cs],
                                        hT[:, 1, 4 * b:4 * b + 4, cs], 4)
                    for k in WO1_STEPS.get(s, ()):
                        prep(l, WO1, k)
                    if s >= 2:
                        n = s - 2
                        u = PJ["wo0"] + n
                        dve.wait_ge(pj_full, l * N_FULL + n_full(u) + 1)
                        dve.tensor_scalar(ost[:, n, 0:512], pj[:, u % 2, :], fo[:, 0, n:n + 1], None,
                                          ALU.mult).then_inc(pj_free, 1)
                dve.tensor_scalar(fo[:, 1, :], yun[:], unsc[:, WO1:WO1 + 1], None, ALU.mult)
                dve.drain()
                dve.wait_ge(gp_in, l * 16 + 16)
                for s in range(NT + 1):
                    if s < NT:
                        u = PJ["wo1"] + s
                        dve.wait_ge(pj_full, l * N_FULL + n_full(u) + 1)
                        dve.tensor_scalar(ost[:, s, 512:1024], pj[:, u % 2, :], fo[:, 1, s:s + 1], None,
                                          ALU.mult).then_inc(pj_free, 1)
                        dve.drain().then_inc(o_ok, 1)
                    if s >= 1:
                        n = s - 1
                        j = NMT + NT + n
                        dve.wait_ge(rstd_ok, l * N_SS + j + 1)
                        dve.scalar_tensor_tensor(ost[:, n, :], ost[:, n, :], rstd[:, j:j + 1], gpost, ALU.mult,
                                                 ALU.mult)
                        dve.drain()
                        dve.wait_ge(xr_in[n % 2], l * 16 * (NT // 2) + 16 * (n // 2) + 16)
                        dve.tensor_tensor(ost[:, n, :], tp[:, n % 2, :], ost[:, n, :], ALU.add).then_inc(out_ok, 1)


LAST = {MKV: PJ["mv"] + NMT - 1, FFRQ: PJ["ffrq"] + 7, RKRV: PJ["rkrv"] + 7, RZ: PJ["rz"] + 7, MQ: PJ["mq"] + 3,
        MZ: MZ_U[-1], FQ: PJ["fq"] + 7, FK: PJ["fk"] + 7, FV: PJ["fv"] + 7, FZ: FZ_U[-1],
        WO0: PJ["wo0"] + 7, WO1: PJ["wo1"] + 7}


def shape_tables():
    import numpy as np
    half = HD // 2
    freqs = (np.float32(10000.0) ** (-np.arange(half, dtype=np.float32) / np.float32(half))).astype(np.float32)
    ang = np.arange(S, dtype=np.float32)[:, None] * freqs[None, :]
    to_rows = lambda a: a.reshape(NT, P, half).transpose(1, 0, 2).reshape(P, NT * half)
    lg = np.log(1.0 - 2.0 ** (-5.0 - np.arange(RET, dtype=np.float64)))
    idx = np.arange(P, dtype=np.float64)
    diff = idx[None, :] - idx[:, None]
    decay = np.where(diff >= 0, np.exp(lg[:, None, None] * np.maximum(diff, 0)), 0.0)
    zeta = np.exp(lg[None, :] * (P - 1 - idx)[:, None])
    xi = np.exp(lg[None, :] * (idx + 1)[:, None])
    dc = np.broadcast_to(np.exp(lg * P)[None, :], (P, RET))
    return np.concatenate([zeta, xi, dc, np.eye(P), to_rows(np.cos(ang)), to_rows(np.sin(ang)),
                           decay.transpose(1, 0, 2).reshape(P, RET * P)], axis=1).astype(np.float32)


_INS = ['x', 'mem', 'w_in', 'b_f', 'w_out', 'w_mem_kv', 'pre_norm', 'post_norm', 'mem_norm']


def kernel(**inputs):
    import numpy as _np
    import concourse.bacc as _bacc
    from concourse import mybir as _mybir
    from concourse.bass_utils import run_bass_kernel_spmd as _run

    nc = _bacc.Bacc("TRN2", target_bir_lowering=False, num_devices=1)
    arrays, args = {}, []
    feed = [(n, _np.ascontiguousarray(inputs[n])) for n in _INS] + [("tables", shape_tables())]
    for name, a in feed:
        arrays[f"in_{name}"] = a
        args.append(nc.dram_tensor(f"in_{name}", a.shape, _mybir.dt.from_np(a.dtype), kind="ExternalInput").ap())
    args.append(nc.dram_tensor("out_0", (1, S, D), _mybir.dt.float32, kind="ExternalOutput").ap())
    build(nc, *args)
    r = _run(nc, [arrays], core_ids=[0])
    return r.results[0]["out_0"]
```
